# Optimizing a Trainium2 kernel written in Bass

```python
import jax, jax.numpy as jnp
from jax import lax
import numpy as np

D_MODEL = 1024
BATCH = 1
SEQ = 512
DEPTH = 2

CHUNK = 64
HEAD_DIM = 64
ROT_DIM = HEAD_DIM // 4
ROPE_THETA = 500000.0
RMS_EPS = 1e-6
LN_EPS = 1e-6
NEG_INF = -1e30

FOX_HEADS = 8
FOX_WIDTH = FOX_HEADS * HEAD_DIM
FOX_BLOCK = 128
DSA_HEADS = 8
DSA_WIDTH = DSA_HEADS * HEAD_DIM
IDX_HEADS = 8
IDX_DIM = 64
DSA_TOPK = 256
DSA_BLOCK = 64
FOX_SPLITS = (FOX_WIDTH, FOX_WIDTH, FOX_WIDTH, FOX_HEADS, FOX_WIDTH)
DSA_SPLITS = (DSA_WIDTH, DSA_WIDTH, DSA_WIDTH, IDX_HEADS * IDX_DIM, IDX_DIM, IDX_HEADS, DSA_WIDTH)
IN0_DIM = sum(FOX_SPLITS) + sum(DSA_SPLITS)
MIX0_WIDTH = FOX_WIDTH + DSA_WIDTH

CHK_HEADS = 16
CHK_WIDTH = CHK_HEADS * HEAD_DIM
CHK_LEFT_CHUNKS = 8
MAX_REL_DIST = 128
CHK_SPLITS = (CHK_WIDTH, CHK_WIDTH, CHK_WIDTH, CHK_WIDTH)
IN1_DIM = sum(CHK_SPLITS)

kernel_name = "hybrid_fox_dsa_chunkattn_sandwich"

def rms_norm(x, g):
    xf = x.astype(jnp.float32)
    y = xf * lax.rsqrt(jnp.mean(xf * xf, axis=-1, keepdims=True) + RMS_EPS)
    return (y * g.astype(jnp.float32)).astype(x.dtype)

def layer_norm(x, g, b):
    xf = x.astype(jnp.float32)
    mu = jnp.mean(xf, axis=-1, keepdims=True)
    xc = xf - mu
    y = xc * lax.rsqrt(jnp.mean(xc * xc, axis=-1, keepdims=True) + LN_EPS)
    return (y * g.astype(jnp.float32) + b.astype(jnp.float32)).astype(x.dtype)

def take_cols(h, sizes):
    out, off = [], 0
    for n in sizes:
        out.append(h[..., off:off + n])
        off += n
    return out

def to_heads(t, n_heads):
    return t.reshape(t.shape[0], t.shape[1], n_heads, HEAD_DIM)

def rope_tables(positions):
    inv_freq = ROPE_THETA ** (-jnp.arange(0, ROT_DIM, 2, dtype=jnp.float32) / ROT_DIM)
    ang = positions.astype(jnp.float32)[..., None] * inv_freq
    return jnp.cos(ang), jnp.sin(ang)

def apply_partial_rope(t, cos, sin):
    half = ROT_DIM // 2
    c = cos[:, :, None, :].astype(t.dtype)
    s = sin[:, :, None, :].astype(t.dtype)
    t1, t2, tp = t[..., :half], t[..., half:ROT_DIM], t[..., ROT_DIM:]
    return jnp.concatenate([t1 * c - t2 * s, t2 * c + t1 * s, tp], axis=-1)

def forgetting_attention(q, k, v, f_logit):
    B, S, H, D = q.shape
    F = jnp.cumsum(jax.nn.log_sigmoid(f_logit.astype(jnp.float32)), axis=1)
    Fh = F.transpose(0, 2, 1)
    scale = D ** -0.5
    key_pos = jnp.arange(S)

    def block(i):
        start = i * FOX_BLOCK
        qb = lax.dynamic_slice_in_dim(q, start, FOX_BLOCK, axis=1)
        Fq = lax.dynamic_slice_in_dim(Fh, start, FOX_BLOCK, axis=2)
        s = jnp.einsum('bqhd,bkhd->bhqk', qb, k, preferred_element_type=jnp.float32) * scale
        s = s + Fq[..., None] - Fh[:, :, None, :]
        q_pos = start + jnp.arange(FOX_BLOCK)
        causal = key_pos[None, :] <= q_pos[:, None]
        s = jnp.where(causal[None, None], s, NEG_INF)
        p = jax.nn.softmax(s, axis=-1)
        return jnp.einsum('bhqk,bkhd->bqhd', p.astype(v.dtype), v)

    out = lax.map(block, jnp.arange(S // FOX_BLOCK))
    return out.transpose(1, 0, 2, 3, 4).reshape(B, S, H * D)

def dsa_attention(q, k, v, iq, ik, iw, top_k):
    B, S, H, D = q.shape
    scale = D ** -0.5
    idx_scale = (IDX_HEADS * IDX_DIM) ** -0.5
    key_pos = jnp.arange(S)

    def block(i):
        start = i * DSA_BLOCK
        qb = lax.dynamic_slice_in_dim(q, start, DSA_BLOCK, axis=1)
        iqb = lax.dynamic_slice_in_dim(iq, start, DSA_BLOCK, axis=1)
        iwb = lax.dynamic_slice_in_dim(iw, start, DSA_BLOCK, axis=1)
        q_pos = start + jnp.arange(DSA_BLOCK)
        limit = (q_pos // CHUNK + 1) * CHUNK
        admissible = key_pos[None, :] < limit[:, None]
        rel = jax.nn.relu(jnp.einsum('bqhd,bkd->bqhk', iqb, ik, preferred_element_type=jnp.float32))
        score = jnp.einsum('bqhk,bqh->bqk', rel, iwb.astype(jnp.float32)) * idx_scale
        score = jnp.where(admissible[None], score, NEG_INF)
        _, sel = lax.top_k(score, top_k)
        ksel = jax.vmap(lambda kb, ib: kb[ib])(k, sel)
        vsel = jax.vmap(lambda vb, ib: vb[ib])(v, sel)
        s = jnp.einsum('bqhd,bqkhd->bhqk', qb, ksel, preferred_element_type=jnp.float32) * scale
        ok = sel < limit[None, :, None]
        s = jnp.where(ok[:, None], s, NEG_INF)
        p = jax.nn.softmax(s, axis=-1)
        return jnp.einsum('bhqk,bqkhd->bqhd', p.astype(v.dtype), vsel)

    out = lax.map(block, jnp.arange(S // DSA_BLOCK))
    return out.transpose(1, 0, 2, 3, 4).reshape(B, S, H * D)

def chunk_band_attention(q, k, v, rel_table):
    B, S, H, D = q.shape
    scale = D ** -0.5
    left = CHK_LEFT_CHUNKS * CHUNK
    band = left + CHUNK
    kp = jnp.pad(k, ((0, 0), (left, 0), (0, 0), (0, 0)))
    vp = jnp.pad(v, ((0, 0), (left, 0), (0, 0), (0, 0)))
    i = jnp.arange(CHUNK)
    j = jnp.arange(band)
    dist = i[:, None] - j[None, :] + left
    bucket = jnp.clip(dist, -MAX_REL_DIST, MAX_REL_DIST) + MAX_REL_DIST
    bias = rel_table[:, bucket].astype(jnp.float32)

    def block(c):
        start = c * CHUNK
        qb = lax.dynamic_slice_in_dim(q, start, CHUNK, axis=1)
        kb = lax.dynamic_slice_in_dim(kp, start, band, axis=1)
        vb = lax.dynamic_slice_in_dim(vp, start, band, axis=1)
        s = jnp.einsum('bqhd,bkhd->bhqk', qb, kb, preferred_element_type=jnp.float32) * scale
        s = s + bias[None]
        valid = j >= left - start
        s = jnp.where(valid[None, None, None, :], s, NEG_INF)
        p = jax.nn.softmax(s, axis=-1)
        return jnp.einsum('bhqk,bkhd->bqhd', p.astype(vb.dtype), vb)

    out = lax.map(block, jnp.arange(S // CHUNK))
    return out.transpose(1, 0, 2, 3, 4).reshape(B, S, H * D)

def even_layer(x, cos, sin, pre_g, post_g, w_in, b_forget, idx_k_g, idx_k_b, w_out, top_k):
    B, S, _ = x.shape
    h = rms_norm(x, pre_g)
    proj = jnp.einsum('bsd,de->bse', h, w_in)
    fq, fk, fv, f_logit, f_gate, dq, dk, dv, iq, ik, iw, d_gate = take_cols(proj, FOX_SPLITS + DSA_SPLITS)
    fox = forgetting_attention(to_heads(fq, FOX_HEADS), to_heads(fk, FOX_HEADS),
                               to_heads(fv, FOX_HEADS), f_logit + b_forget)
    fox = fox * jax.nn.silu(f_gate)
    dq = apply_partial_rope(to_heads(dq, DSA_HEADS), cos, sin)
    dk = apply_partial_rope(to_heads(dk, DSA_HEADS), cos, sin)
    dv = to_heads(dv, DSA_HEADS)
    iq = apply_partial_rope(iq.reshape(B, S, IDX_HEADS, IDX_DIM), cos, sin)
    ik = apply_partial_rope(layer_norm(ik, idx_k_g, idx_k_b)[:, :, None, :], cos, sin)[:, :, 0, :]
    dsa = dsa_attention(dq, dk, dv, iq, ik, iw, top_k) * jax.nn.silu(d_gate)
    y = jnp.einsum('bse,ed->bsd', jnp.concatenate([fox, dsa], axis=-1), w_out)
    return x + rms_norm(y, post_g)

def odd_layer(x, pre_g, post_g, w_in, rel_table, w_out):
    h = rms_norm(x, pre_g)
    proj = jnp.einsum('bsd,de->bse', h, w_in)
    cq, ck, cv, c_gate = take_cols(proj, CHK_SPLITS)
    att = chunk_band_attention(to_heads(cq, CHK_HEADS), to_heads(ck, CHK_HEADS),
                               to_heads(cv, CHK_HEADS), rel_table)
    y = jnp.einsum('bse,ed->bsd', att * jax.nn.silu(c_gate), w_out)
    return x + rms_norm(y, post_g)

def setup_inputs(seed: int = 0) -> dict:
    key = jax.random.key(seed)
    ks = jax.random.split(key, 12)
    n_even = (DEPTH + 1) // 2
    n_odd = DEPTH // 2
    f32 = jnp.float32
    x = jax.random.normal(ks[0], (BATCH, SEQ, D_MODEL), f32)
    positions = jnp.broadcast_to(jnp.arange(SEQ, dtype=jnp.int32), (BATCH, SEQ))
    pre_norm_g = 1.0 + 0.05 * jax.random.normal(ks[1], (DEPTH, D_MODEL), f32)
    post_norm_g = 1.0 + 0.05 * jax.random.normal(ks[2], (DEPTH, D_MODEL), f32)
    w_in_even = jax.random.normal(ks[3], (n_even, D_MODEL, IN0_DIM), f32) * D_MODEL ** -0.5
    b_forget = jax.random.uniform(ks[4], (n_even, FOX_HEADS), f32, minval=1.0, maxval=5.0)
    idx_k_g = 1.0 + 0.05 * jax.random.normal(ks[5], (n_even, IDX_DIM), f32)
    idx_k_b = 0.02 * jax.random.normal(ks[6], (n_even, IDX_DIM), f32)
    w_out_even = jax.random.normal(ks[7], (n_even, MIX0_WIDTH, D_MODEL), f32) * MIX0_WIDTH ** -0.5
    w_in_odd = jax.random.normal(ks[8], (n_odd, D_MODEL, IN1_DIM), f32) * D_MODEL ** -0.5
    rel_bias = 0.5 * jax.random.normal(ks[9], (n_odd, CHK_HEADS, 2 * MAX_REL_DIST + 1), f32)
    w_out_odd = jax.random.normal(ks[10], (n_odd, CHK_WIDTH, D_MODEL), f32) * CHK_WIDTH ** -0.5
    return {"x": x, "positions": positions, "pre_norm_g": pre_norm_g, "post_norm_g": post_norm_g,
            "w_in_even": w_in_even, "b_forget": b_forget, "idx_k_g": idx_k_g, "idx_k_b": idx_k_b,
            "w_out_even": w_out_even, "w_in_odd": w_in_odd, "rel_bias": rel_bias, "w_out_odd": w_out_odd}

def reference(x, positions, pre_norm_g, post_norm_g, w_in_even, b_forget, idx_k_g, idx_k_b,
              w_out_even, w_in_odd, rel_bias, w_out_odd):
    seq = x.shape[1]
    top_k = min(DSA_TOPK, seq // 4)
    cos, sin = rope_tables(positions)
    for layer in range(DEPTH):
        if layer % 2 == 0:
            e = layer // 2
            x = even_layer(x, cos, sin, pre_norm_g[layer], post_norm_g[layer], w_in_even[e],
                           b_forget[e], idx_k_g[e], idx_k_b[e], w_out_even[e], top_k)
        else:
            o = layer // 2
            x = odd_layer(x, pre_norm_g[layer], post_norm_g[layer], w_in_odd[o], rel_bias[o], w_out_odd[o])
    return x


_drawn_inputs = setup_inputs


def setup_inputs(seed=0):
    import zlib

    import numpy as np

    out = dict(_drawn_inputs(seed))
    spreads = {}
    factors = {}
    for name, (base, spread) in spreads.items():
        noise = np.random.default_rng([zlib.crc32(name.encode()), seed]).standard_normal(out[name].shape)
        drawn = base * np.exp(spread * noise) if base else spread * noise
        out[name] = __import__('jax').numpy.asarray(drawn.astype(out[name].dtype))
    for name, factor in factors.items():
        out[name] = (out[name] * factor).astype(out[name].dtype)
    return out
```

```python
from contextlib import ExitStack, contextmanager

import numpy as np

import concourse.bass as bass
from concourse import mybir

F32 = mybir.dt.float32
F32R = mybir.dt.float32r
BF16 = mybir.dt.bfloat16
I32 = mybir.dt.int32
ALU = mybir.AluOpType
ACT = mybir.ActivationFunctionType
AX = mybir.AxisListType

P = 128
D = 1024
S = 512
KT = D // P
NT = S // P
HD = 64
ROT = HD // 4
PAIRS = 8
FOX_PAIRS = 4
IDX_UNITS = 4
IDX_HEADS = 8
SMALL = 80
F_ROW, IW_ROW = 64, 72
TOPK = min(256, S // 4)
ROUNDS = TOPK // 8
CHUNK = 64
REL = 128
TAB = 2 * REL + 1
EXT = 640
THETA = 500000.0
EPS = 1e-6
NEG = -1e30
TAKEN = -3e38
BIG = 3e38
SCALE = HD ** -0.5
IDX_SCALE = (IDX_HEADS * HD) ** -0.5
OFF = [0, 128, 384, 768]
PACK = 1280
W_OFF = [None, 0, 256, 640]
W_PACK = 1152
KOFF = [0, 512, 896, 1152]
TWO_PI = 2 * np.pi
PI_HI = 6.28125
PI_MID = float(np.float32(0.0019350051879882812))
PI_LO = float(np.float32(TWO_PI - PI_HI - PI_MID))
PI_MAX = 3.1415925
ROUND_MAGIC = 12582912.0
SWAP = [i + 8 if i < 8 else i - 8 if i < 16 else i for i in range(32)]

GROUPS = [(0, [3]), (1, [3]), (0, [2]), (1, [2]), (0, [1, 0]), (1, [1, 0])]


class Steps:

    def __init__(self, eng, sem):
        self.eng, self.sem, self.base, self.n = eng, sem, 0, 0

    def mark(self, ins):
        ins.then_inc(self.sem, 1)
        self.n += 1
        return self.base + self.n

    def wait(self, count):
        self.eng.wait_ge(self.sem, count)

    def done(self, ins):
        self.wait(self.mark(ins))

    @contextmanager
    def loop(self, count, per_turn):
        base, n = self.base, self.n
        with self.eng.Fori(0, count) as i:
            self.base, self.n = base + n + i * per_turn, 0
            yield i
            assert self.n == per_turn, self.n
        self.base, self.n = base + n + count * per_turn, 0


def wait_past(eng, semaphore, count):
    if not isinstance(count, int) or count > 0:
        eng.wait_ge(semaphore, count)


def alone(eng):
    eng.nop(nofuse=True)


def trunk_program(nc, x, positions, pre_g, post_g, w_units, w_small, b_forget, idx_g, idx_b,
                  rel_bias, rope_consts, out, neg_f_dram, ext_dram):
    with ExitStack() as ctx:
        def sb(name, shape, dt=F32):
            return ctx.enter_context(nc.sbuf_tensor(name, shape, dt))

        def sem(name):
            return ctx.enter_context(nc.semaphore(name))

        bank = [ctx.enter_context(nc.psum_tensor(f"bank{i}", [P, S], F32)) for i in range(8)]
        score_bank = bank[0:3]
        proj_bank = bank[3:5]
        pt_bank = bank[5:7]
        pv_bank = bank[7]

        xt = sb("xt", [P, NT, D])
        h_hi = sb("h_hi", [P, KT, S], F32R)
        h_lo = sb("h_lo", [P, KT, S], F32R)
        mix_hi = sb("mix_hi", [P, PAIRS, S], F32R)
        mix_lo = sb("mix_lo", [P, PAIRS, S], F32R)
        w_raw = sb("w_raw", [P, 4, D])
        w_hi = sb("w_hi", [P, 4, D], F32R)
        w_lo = sb("w_lo", [P, 4, D], F32R)
        q_hi = sb("q_hi", [P, S], F32R)
        q_lo = sb("q_lo", [P, S], F32R)
        k_hi = sb("k_hi", [P, S], F32R)
        k_lo = sb("k_lo", [P, S], F32R)
        v_t = sb("v_t", [P, S])
        v = sb("v", [P, NT, P])
        tanh_gate = sb("tanh_gate", [P, 2, S])
        tanh_g, gate = tanh_gate[:, 0, :], tanh_gate[:, 1, :]
        probs = sb("probs", [P, 2, PACK])
        probs_t = sb("probs_t", [P, 2, PACK])
        mix = sb("mix", [P, S])
        bias = sb("bias", [P, 2, S])
        neg_max = sb("neg_max", [P, 8])
        row_sum = sb("row_sum", [P, 8])
        row_inv = sb("row_inv", [P, 8])
        rope_a = sb("rope_a", [P, S])
        rope_b = sb("rope_b", [P, S])
        cos_t = sb("cos_t", [P, S])
        sin_t = sb("sin_t", [P, S])
        work = sb("work", [P, W_PACK])
        sel_bias = sb("sel_bias", [P, PACK])
        best8 = sb("best8", [P, 3, 8])
        ws_hi = sb("ws_hi", [P, KT, SMALL], F32R)
        ws_lo = sb("ws_lo", [P, KT, SMALL], F32R)
        small_tok = sb("small_tok", [P, NT, SMALL])
        ik_stat = sb("ik_stat", [P, 4, NT])
        ik_gb = sb("ik_gb", [P, 2])
        b_f = sb("b_f", [SMALL, 1])
        tab = sb("tab", [16, TAB])
        g_pre = sb("g_pre", [P, D])
        g_post = sb("g_post", [P, D])
        sum_sq = sb("sum_sq", [P, 2, 2, NT, 2])
        mean_sq = sb("mean_sq", [P, 2, 2, NT])
        rstd = sb("rstd", [P, 2, 2, NT])
        half_neg = sb("half_neg", [P, NT])
        ident = sb("ident", [P, P])
        ident_b = sb("ident_b", [P, P], BF16)
        causal_b = sb("causal_b", [P, P], BF16)
        chunk_b = sb("chunk_b", [P, P], BF16)
        rope_c = sb("rope_c", [P, 4])

        squares = tanh_gate[:, :, :].rearrange("p a s -> p (a s)")
        pos_i = v_t[:, :].bitcast(I32)
        small = mix[0:SMALL, :]
        ws_raw = bias[:, :, :].rearrange("p h s -> p (h s)")[:, 0:KT * SMALL].rearrange("p (k c) -> p k c", k=KT)
        normed = probs_t[:, :, 0:D]
        y_normed = probs[:, :, 0:D]
        relu = probs_t[:, :, 0:S]
        iq_hi, iq_lo = mix_hi[:, 0:4, :], mix_lo[:, 0:4, :]
        ik_hi, ik_lo = mix_hi[:, 4, :], mix_lo[:, 4, :]
        ik_c = probs[:, 0, 0:NT * HD].rearrange("p (t d) -> p t d", t=NT)
        ik_sq = probs[:, 0, 256:256 + NT * HD].rearrange("p (t d) -> p t d", t=NT)
        ik_dup = probs[:, 0, 512:512 + NT * P].rearrange("p (t c d) -> p t c d", t=NT, c=2)
        ik_gained = probs[:, 1, 0:S]
        angle, turns, reduced = squares[:, 0:S], squares[:, S:D], rope_a[:, :]
        fz, fa = (probs[F_ROW:F_ROW + 8, 1, a:a + S] for a in (512, 0))
        ones8 = rope_b[F_ROW:F_ROW + 8, :]
        ext = g_post[0:16, 0:EXT]

        x_landed = [sem(f"x_landed{t}") for t in range(NT)]
        raw_landed = [sem(f"raw_landed{j}") for j in range(4)]
        ws_landed = sem("ws_landed")
        consts_landed = sem("consts_landed")
        gpre_landed = sem("gpre_landed")
        gpost_landed = sem("gpost_landed")
        bias_landed = sem("bias_landed")
        neg_f_stored = sem("neg_f_stored")
        ext_stored = sem("ext_stored")
        out_stored = sem("out_stored")
        consts_ready = sem("consts_ready")
        sumsq_ready = sem("sumsq_ready")
        rstd_ready = sem("rstd_ready")
        normed_ready = sem("normed_ready")
        xt_ready = sem("xt_ready")
        h_hi_ready = sem("h_hi_ready")
        h_lo_ready = sem("h_lo_ready")
        y_ready = sem("y_ready")
        ysq_ready = sem("ysq_ready")
        yrstd_ready = sem("yrstd_ready")
        y_read = sem("y_read")
        x_added = sem("x_added")
        w_hi_ready = sem("w_hi_ready")
        w_lo_ready = sem("w_lo_ready")
        unit_used = sem("unit_used")
        ws_hi_ready = sem("ws_hi_ready")
        ws_lo_ready = sem("ws_lo_ready")
        q_hi_ready = sem("q_hi_ready")
        q_ready = sem("q_ready")
        k_hi_ready = sem("k_hi_ready")
        k_ready = sem("k_ready")
        roped = sem("roped")
        v_staged = sem("v_staged")
        vt_ready = sem("vt_ready")
        v_ready = sem("v_ready")
        tanh_ready = sem("tanh_ready")
        gate_ready = sem("gate_ready")
        scores_ready = sem("scores_ready")
        scored = sem("scored")
        exp_ready = sem("exp_ready")
        inv_ready = sem("inv_ready")
        probs_ready = sem("probs_ready")
        pt_ready = sem("pt_ready")
        pt_read = sem("pt_read")
        pv_done = sem("pv_done")
        mixed = sem("mixed")
        mix_hi_ready = sem("mix_hi_ready")
        mix_lo_ready = sem("mix_lo_ready")
        small_done = sem("small_done")
        small_ready = sem("small_ready")
        small_t_ready = sem("small_t_ready")
        ik_var_ready = sem("ik_var_ready")
        ik_rstd_ready = sem("ik_rstd_ready")
        ik_dup_ready = sem("ik_dup_ready")
        ik_t_ready = sem("ik_t_ready")
        iq_done = sem("iq_done")
        i_roped = sem("i_roped")
        i_hi_ready = sem("i_hi_ready")
        i_lo_ready = sem("i_lo_ready")
        idx_ready = sem("idx_ready")
        relu_ready = sem("relu_ready")
        relu_used = sem("relu_used")
        angle_ready = sem("angle_ready")
        sine_ready = sem("sine_ready")
        fz_ready = sem("fz_ready")
        fl_ready = sem("fl_ready")
        neg_f_ready = sem("neg_f_ready")
        ext_ready = sem("ext_ready")
        dve_steps = sem("dve_steps")
        act_steps = sem("act_steps")
        pool_steps = sem("pool_steps")

        block = ctx.enter_context(nc.Block())

        @block.sync
        def _(sp):
            sp.dma_start(ws_raw, w_small.rearrange("p (k c) -> p k c", k=KT)).then_inc(ws_landed, 16)
            for j in range(4):
                sp.dma_start(w_raw[:, j, :], w_units[j]).then_inc(raw_landed[j], 16)

            def load_round(r, first):
                for j in range(4):
                    sp.wait_ge(w_lo_ready, 4 * (r - 1) + j + 1)
                    sp.dma_start(w_raw[:, j, :], w_units[first + j]).then_inc(raw_landed[j], 16)

            with sp.Fori(0, 10) as i:
                load_round(i + 1, 4 * i + 4)
            with sp.Fori(0, 12) as i:
                load_round(i + 11, 4 * i + 36)
            with sp.Fori(0, 2) as i:
                load_round(i + 23, 4 * i + 76)
            for t in range(NT):
                sp.wait_ge(x_added, NT + t + 1)
                sp.dma_start(out[t * P:(t + 1) * P, :], xt[:, t, :]).then_inc(out_stored, 16)
            sp.wait_ge(out_stored, 16 * NT)

        @block.gpsimd
        def _(pool):
            st = Steps(pool, pool_steps)
            pool.dma_start(g_pre[:, :], pre_g[0:1, :].partition_broadcast(P)).then_inc(gpre_landed, 16)
            pool.memset(half_neg[:, :], -0.5)
            pool.memset(sel_bias[:, 0:P], 0.0)
            pool.memset(ident[:, :], 0.0)
            pool.memset(causal_b[:, :], 0.0)
            st.done(pool.memset(chunk_b[:, :], 0.0))
            st.done(pool.affine_select(out=ident[:, :], in_=ident[:, :], compare_op=ALU.not_equal, fill=1.0,
                                       base=0, pattern=[[-1, P]], channel_multiplier=1))
            pool.affine_select(out=causal_b[:, :], in_=causal_b[:, :], compare_op=ALU.is_ge, fill=NEG,
                               base=0, pattern=[[-1, P]], channel_multiplier=1)
            pool.memset(chunk_b[0:CHUNK, CHUNK:P], NEG)
            pool.memset(sel_bias[0:CHUNK, CHUNK:P], NEG)
            pool.tensor_copy(ident_b[:, :], ident[:, :]).then_inc(consts_ready, 1)
            pool.dma_start(rope_c[:, :], rope_consts).then_inc(consts_landed, 16)
            pool.dma_start(pos_i, positions.partition_broadcast(P)).then_inc(consts_landed, 16)
            for half in range(2):
                for col, src in ((0, idx_g), (1, idx_b)):
                    pool.dma_start(ik_gb[HD * half:HD * half + HD, col:col + 1], src).then_inc(consts_landed, 16)
            pool.dma_start(b_f[F_ROW:F_ROW + 8, :], b_forget).then_inc(consts_landed, 16)
            pool.dma_start(tab[:, :], rel_bias).then_inc(consts_landed, 16)

            def x_rstd(layer, t):
                pool.wait_ge(sumsq_ready, NT * layer + t + 1)
                st.done(pool.tensor_scalar(mean_sq[:, layer, 0, t:t + 1], sum_sq[:, layer, 0, t, 0:1],
                                           1.0 / D, EPS, ALU.mult, ALU.add))
                pool.tensor_tensor(rstd[:, layer, 0, t:t + 1], mean_sq[:, layer, 0, t:t + 1],
                                   half_neg[:, 0:1], ALU.pow).then_inc(rstd_ready, 1)

            def y_rstd(layer, t):
                pool.wait_ge(ysq_ready, NT * layer + t + 1)
                both = sum_sq[:, layer, 1, t, :]
                st.done(pool.tensor_tensor(both[:, 0:1], both[:, 0:1], both[:, 1:2], ALU.add))
                st.done(pool.tensor_scalar(mean_sq[:, layer, 1, t:t + 1], both[:, 0:1],
                                           1.0 / D, EPS, ALU.mult, ALU.add))
                pool.tensor_tensor(rstd[:, layer, 1, t:t + 1], mean_sq[:, layer, 1, t:t + 1],
                                   half_neg[:, 0:1], ALU.pow).then_inc(yrstd_ready, 1)

            def normalise(g):
                for h in range(2):
                    pool.wait_ge(inv_ready, 2 * g + h + 1)
                    alone(pool)
                    for t in (3, 2, 1, 0):
                        seg = probs[:, h, OFF[t]:OFF[t] + (t + 1) * P]
                        pool.tensor_scalar(seg, seg, row_inv[:, 4 * h + t:4 * h + t + 1], 0.0,
                                           ALU.mult, ALU.add).then_inc(probs_ready, 1)

            def load_fox_bias(pair):
                src = neg_f_dram[pair].rearrange("(o n) -> o n", o=1).partition_broadcast(P)
                pool.dma_start(bias[:, :, :].rearrange("p h s -> p (h s)"), src).then_inc(bias_landed, 16)

            def load_chk_bias(pair):
                rows = ext_dram[pair].rearrange("(h n) -> h n", h=2)[:, P - 1:P - 1 + P * (EXT - 1)]
                src = rows.rearrange("h (p w) -> p h w", w=EXT - 1)[:, :, 0:S]
                pool.dma_start(bias[:, :, :], src).then_inc(bias_landed, 16)

            for t in range(NT):
                x_rstd(0, t)
            pool.wait_ge(normed_ready, NT)
            pool.dma_start(g_pre[:, :], pre_g[1:2, :].partition_broadcast(P)).then_inc(gpre_landed, 16)
            pool.wait_ge(ik_var_ready, 1)
            pool.tensor_tensor(ik_stat[:, 2, :], ik_stat[:, 1, :], half_neg[:, :], ALU.pow)\
                .then_inc(ik_rstd_ready, 1)
            pool.wait_ge(ext_ready, 1)
            pool.dma_start(ext_dram.rearrange("a (h p w) -> (a h) p w", h=2, p=P),
                           ext.rearrange("h (o w) -> h o w", o=1).to_broadcast([16, P, EXT]))\
                .then_inc(ext_stored, 16)
            pool.wait_ge(neg_f_ready, 1)
            pool.dma_start(neg_f_dram.rearrange("a (b s) -> (a b) s", b=2), small[F_ROW:F_ROW + 8, :])\
                .then_inc(neg_f_stored, 16)
            pool.wait_ge(neg_f_stored, 16)
            load_fox_bias(0)
            with pool.Fori(0, 3) as g:
                normalise(g)
                pool.wait_ge(scored, 6 * g + 6)
                load_fox_bias(g + 1)
            with pool.Fori(3, 8) as g:
                normalise(g)
            pool.wait_ge(ext_stored, 16)
            pool.dma_start(g_post[:, :], post_g[0:1, :].partition_broadcast(P)).then_inc(gpost_landed, 16)
            pool.wait_ge(scored, 24)
            load_chk_bias(0)
            for t in range(2):
                y_rstd(0, t)
            for t in range(2):
                x_rstd(1, t)
            for t in range(2, NT):
                y_rstd(0, t)
            pool.wait_ge(y_read, NT)
            pool.dma_start(g_post[:, :], post_g[1:2, :].partition_broadcast(P)).then_inc(gpost_landed, 16)
            for t in range(2, NT):
                x_rstd(1, t)
            with pool.Fori(0, 7) as i:
                normalise(i + 8)
                pool.wait_ge(scored, 6 * i + 54)
                load_chk_bias(i + 1)
            normalise(15)
            for t in range(NT):
                y_rstd(1, t)

        @block.scalar
        def _(act):
            st = Steps(act, act_steps)
            for t in range(NT):
                act.dma_start(xt[:, t, :], x[t * P:(t + 1) * P, :]).then_inc(x_landed[t], 16)

            def split_hi(r, j, first=False):
                act.wait_ge(raw_landed[j], 16 * r + 16)
                if not first:
                    act.wait_ge(unit_used, 4 * r + j - 3)
                act.activation(w_hi[:, j, :], w_raw[:, j, :], ACT.Copy).then_inc(w_hi_ready, 1)

            def x_square(layer, t):
                if layer == 0:
                    act.wait_ge(x_landed[t], 16)
                else:
                    act.wait_ge(x_added, t + 1)
                if layer or t:
                    act.wait_ge(sumsq_ready, NT * layer + t)
                if layer:
                    act.wait_ge(ysq_ready, 2 if t < 2 else 4)
                act.activation(squares[:, :], xt[:, t, :], ACT.Square,
                               accum_out=sum_sq[:, layer, 0, t, 0:1]).then_inc(sumsq_ready, 1)

            def h_high(layer, t):
                for half in range(2):
                    n = 2 * (NT * layer + t) + half
                    act.wait_ge(xt_ready, n + 1)
                    act.activation(h_hi[:, 4 * half:4 * half + 4, t * P:(t + 1) * P],
                                   bank[2 * (t % 2) + half][:, :].rearrange("p (k s) -> p k s", k=4),
                                   ACT.Copy).then_inc(h_hi_ready, 1)

            def y_square(layer, t):
                if t % 2 == 0:
                    act.wait_ge(y_ready, 2 * layer + t // 2 + 1)
                else:
                    act.wait_ge(unit_used, 4 * ((9, 21)[layer] + t) + 4)
                if layer or t:
                    act.wait_ge(ysq_ready, NT * layer + t)
                if t in (0, 2):
                    act.wait_ge(sumsq_ready, (NT, NT + 2, 2 * NT, 2 * NT)[2 * layer + t // 2])
                for half in range(2):
                    ins = act.activation(squares[:, half * S:(half + 1) * S], bank[2 * t + half][:, :],
                                         ACT.Square, accum_out=sum_sq[:, layer, 1, t, half:half + 1])
                ins.then_inc(ysq_ready, 1)

            def exps(g, n):
                h, tiles = GROUPS[n]
                for t in tiles:
                    act.wait_ge(scored, 6 * g + n + 1)
                    seg = probs[:, h, OFF[t]:OFF[t] + (t + 1) * P]
                    act.activation(seg, seg, ACT.Exp, bias=neg_max[:, 4 * h + t:4 * h + t + 1], scale=-1.0,
                                   accum_out=row_sum[:, 4 * h + t:4 * h + t + 1]).then_inc(exp_ready, 1)

            def q_high(a, r, rope):
                if not rope:
                    act.wait_ge(unit_used, 4 * r + 1)
                wait_past(act, scores_ready, 6 * a)
                if rope:
                    act.wait_ge(roped, 2 * (a - 4) + 1)
                    act.activation(q_hi[:, :], rope_b[:, :], ACT.Copy).then_inc(q_hi_ready, 1)
                else:
                    act.activation(q_hi[:, :], proj_bank[0][:, :], ACT.Copy, scale=SCALE).then_inc(q_hi_ready, 1)

            def k_high(a, r, rope):
                if rope:
                    act.wait_ge(roped, 2 * (a - 4) + 2)
                    act.activation(k_hi[:, :], rope_b[:, :], ACT.Copy).then_inc(k_hi_ready, 1)
                else:
                    act.wait_ge(unit_used, 4 * r + 2)
                    act.activation(k_hi[:, :], proj_bank[1][:, :], ACT.Copy).then_inc(k_hi_ready, 1)

            def v_stage(a, r):
                act.wait_ge(unit_used, 4 * r + 3)
                wait_past(act, vt_ready, a)
                act.activation(v_t[:, :], proj_bank[0][:, :], ACT.Copy).then_inc(v_staged, 1)

            def gate_tanh(a, r):
                act.wait_ge(unit_used, 4 * r + 4)
                wait_past(act, gate_ready, a)
                act.activation(tanh_g, proj_bank[1][:, :], ACT.Tanh, scale=0.5).then_inc(tanh_ready, 1)

            def v_copy(a):
                act.wait_ge(vt_ready, a + 1)
                wait_past(act, pv_done, 2 * a)
                act.activation(v[:, :, :], score_bank[2][:, :].rearrange("p (t d) -> p t d", t=NT),
                               ACT.Copy).then_inc(v_ready, 1)

            def copy_probs_t(g, h):
                wait_past(act, pv_done, 2 * g)
                for n in range(3):
                    act.wait_ge(pt_ready, 6 * g + 3 * h + n + 1)
                    a, b = (0, 512, 896, 1280)[n:n + 2]
                    act.activation(probs_t[:, h, a:b], pt_bank[(3 * h + n) % 2][:, 0:b - a], ACT.Copy)\
                        .then_inc(pt_read, 1)

            def mix_high(g, pair):
                act.wait_ge(mixed, g + 1)
                act.activation(mix_hi[:, pair, :], mix[:, :], ACT.Copy).then_inc(mix_hi_ready, 1)

            def project(a, r, rope):
                split_hi(r + 1, 0)
                q_high(a, r, rope)
                split_hi(r + 1, 1)
                k_high(a, r, rope)
                v_stage(a, r)
                split_hi(r + 1, 2)
                gate_tanh(a, r)
                split_hi(r + 1, 3)
                v_copy(a)

            def body(g, pair, nxt, shift=0):
                r = g + 2 + shift
                for n in range(3):
                    exps(g, n)
                if nxt:
                    split_hi(r + 1, 0)
                for n in range(3, 6):
                    exps(g, n)
                if nxt:
                    q_high(g + 1, r, nxt == "dsa")
                    split_hi(r + 1, 1)
                    k_high(g + 1, r, nxt == "dsa")
                copy_probs_t(g, 0)
                if nxt:
                    v_stage(g + 1, r)
                    split_hi(r + 1, 2)
                copy_probs_t(g, 1)
                if nxt:
                    gate_tanh(g + 1, r)
                    split_hi(r + 1, 3)
                    v_copy(g + 1)
                mix_high(g, pair)

            x_square(0, 0)
            x_square(0, 1)
            act.wait_ge(ws_landed, 16)
            act.activation(ws_hi[:, :, :], ws_raw, ACT.Copy).then_inc(ws_hi_ready, 1)
            x_square(0, 2)
            x_square(0, 3)
            split_hi(0, 0, first=True)
            h_high(0, 0)
            h_high(0, 1)
            split_hi(0, 1, first=True)
            h_high(0, 2)
            h_high(0, 3)
            split_hi(0, 2, first=True)
            split_hi(0, 3, first=True)
            act.wait_ge(angle_ready, 1)
            act.activation(sin_t[:, :], rope_b[:, :], ACT.Sin).then_inc(sine_ready, 1)
            act.wait_ge(angle_ready, 2)
            act.activation(cos_t[:, :], rope_a[:, :], ACT.Sin).then_inc(sine_ready, 1)
            act.wait_ge(small_done, 1)
            act.activation(small, bank[2][0:SMALL, :], ACT.Copy).then_inc(small_ready, 1)
            act.wait_ge(fz_ready, 1)
            st.done(act.activation(fa, fz, ACT.Abs))
            st.done(act.activation(fa, fa, ACT.Exp, scale=-1.0))
            act.activation(fa, fa, ACT.Ln, bias=1.0).then_inc(fl_ready, 1)
            for j in range(IDX_UNITS):
                split_hi(1, j)
                act.wait_ge(i_roped, j + 1)
                act.activation(iq_hi[:, j, :], rope_b[:, :], ACT.Copy).then_inc(i_hi_ready, 1)
            act.wait_ge(i_roped, IDX_UNITS + 1)
            act.activation(ik_hi, rope_b[:, :], ACT.Copy).then_inc(i_hi_ready, 1)

            def relu_step(s):
                t = s % 3 + 1
                act.wait_ge(idx_ready, s + 1)
                if s >= 2:
                    act.wait_ge(relu_used, s - 1)
                w = (t + 1) * P
                act.activation(relu[:, s % 2, 0:w], score_bank[s % 3][:, 0:w], ACT.Relu).then_inc(relu_ready, 1)

            split_hi(2, 0)
            q_high(0, 1, False)
            for s in range(0, 8):
                relu_step(s)
            split_hi(2, 1)
            k_high(0, 1, False)
            for s in range(8, 16):
                relu_step(s)
            v_stage(0, 1)
            split_hi(2, 2)
            for s in range(16, 24):
                relu_step(s)
            gate_tanh(0, 1)
            split_hi(2, 3)
            v_copy(0)

            body(0, 0, "fox")
            with act.Fori(1, 3) as g:
                body(g, g, "fox")
            with act.Fori(3, 7) as g:
                body(g, g, "dsa")
            body(7, 7, None)

            def out_norms(layer, r, last):
                for j in range(4):
                    split_hi(r + 1, j)
                for j in range(4):
                    split_hi(r + 2, j)
                y_square(layer, 0)
                y_square(layer, 1)
                split_hi(r + 3, 0)
                if not last:
                    x_square(1, 0)
                split_hi(r + 3, 1)
                if not last:
                    x_square(1, 1)
                split_hi(r + 3, 2)
                split_hi(r + 3, 3)
                if not last:
                    h_high(1, 0)
                    h_high(1, 1)
                    for j in range(4):
                        split_hi(r + 4, j)
                y_square(layer, 2)
                y_square(layer, 3)
                if not last:
                    x_square(1, 2)
                    x_square(1, 3)
                    h_high(1, 2)
                    h_high(1, 3)

            out_norms(0, 9, False)
            project(8, 13, False)
            with act.Fori(0, 7) as i:
                body(i + 8, i, "chk", 4)
            body(15, 7, None)
            out_norms(1, 21, True)

        @block.vector
        def _(dve):
            st = Steps(dve, dve_steps)

            def split_lo(r, j):
                dve.wait_ge(w_hi_ready, 4 * r + j + 1)
                dve.tensor_tensor(w_lo[:, j, :], w_raw[:, j, :], w_hi[:, j, :].bitcast(F32), ALU.subtract)\
                    .then_inc(w_lo_ready, 1)

            def x_scale(layer, t):
                dve.wait_ge(rstd_ready, NT * layer + t + 1)
                if t == 0:
                    dve.wait_ge(gpre_landed, 16 * (layer + 1))
                if t >= 2:
                    dve.wait_ge(xt_ready, 2 * (NT * layer + t - 1))
                dve.scalar_tensor_tensor(out=normed[:, t % 2, :], in0=xt[:, t, :], scalar=rstd[:, layer, 0, t:t + 1],
                                         in1=g_pre[:, :], op0=ALU.mult, op1=ALU.mult).then_inc(normed_ready, 1)

            def h_low(layer, t):
                for half in range(2):
                    dve.wait_ge(h_hi_ready, 2 * (NT * layer + t) + half + 1)
                    ks = slice(4 * half, 4 * half + 4)
                    dve.tensor_tensor(h_lo[:, ks, t * P:(t + 1) * P],
                                      bank[2 * (t % 2) + half][:, :].rearrange("p (k s) -> p k s", k=4),
                                      h_hi[:, ks, t * P:(t + 1) * P].bitcast(F32),
                                      ALU.subtract).then_inc(h_lo_ready, 1)

            def y_scale(layer, t):
                dve.wait_ge(yrstd_ready, NT * layer + t + 1)
                if t == 0:
                    dve.wait_ge(gpost_landed, 16 * (layer + 1))
                for half in range(2):
                    cols = slice(half * S, (half + 1) * S)
                    ins = dve.scalar_tensor_tensor(out=y_normed[:, t % 2, cols], in0=bank[2 * t + half][:, :],
                                                   scalar=rstd[:, layer, 1, t:t + 1], in1=g_post[:, cols],
                                                   op0=ALU.mult, op1=ALU.mult)
                ins.then_inc(y_read, 1)
                dve.wait_ge(y_read, NT * layer + t + 1)
                dve.tensor_tensor(xt[:, t, :], xt[:, t, :], y_normed[:, t % 2, :], ALU.add).then_inc(x_added, 1)

            def rope(src, scale):
                alone(dve)
                st.done(dve.stream_shuffle(rope_a[:, :], src, SWAP))
                a = st.mark(dve.scalar_tensor_tensor(out=rope_a[:, :], in0=rope_a[:, :], scalar=scale,
                                                     in1=sin_t[:, :], op0=ALU.mult, op1=ALU.mult))
                b = st.mark(dve.scalar_tensor_tensor(out=rope_b[:, :], in0=src, scalar=scale, in1=cos_t[:, :],
                                                     op0=ALU.mult, op1=ALU.mult))
                st.wait(b)
                return dve.tensor_tensor(rope_b[:, :], rope_b[:, :], rope_a[:, :], ALU.add)

            def q_low(a, r, rotary):
                if rotary:
                    dve.wait_ge(unit_used, 4 * r + 1)
                    rope(proj_bank[0][:, :], SCALE).then_inc(roped, 1)
                    dve.wait_ge(roped, 2 * (a - 4) + 1)
                dve.wait_ge(q_hi_ready, a + 1)
                if rotary:
                    dve.tensor_tensor(q_lo[:, :], rope_b[:, :], q_hi[:, :].bitcast(F32), ALU.subtract)\
                        .then_inc(q_ready, 1)
                else:
                    dve.scalar_tensor_tensor(out=q_lo[:, :], in0=proj_bank[0][:, :], scalar=SCALE,
                                             in1=q_hi[:, :].bitcast(F32), op0=ALU.mult, op1=ALU.subtract)\
                        .then_inc(q_ready, 1)

            def k_low(a, r, rotary):
                src = proj_bank[1]
                if rotary:
                    dve.wait_ge(unit_used, 4 * r + 2)
                    dve.wait_ge(q_ready, a + 1)
                    rope(src[:, :], 1.0).then_inc(roped, 1)
                    dve.wait_ge(roped, 2 * (a - 4) + 2)
                    src = rope_b
                dve.wait_ge(k_hi_ready, a + 1)
                dve.tensor_tensor(k_lo[:, :], src[:, :], k_hi[:, :].bitcast(F32), ALU.subtract)\
                    .then_inc(k_ready, 1)

            def gate_make(a):
                dve.wait_ge(tanh_ready, a + 1)
                wait_past(dve, mixed, a)
                dve.scalar_tensor_tensor(out=gate, in0=tanh_g, scalar=1.0, in1=proj_bank[1][:, :],
                                         op0=ALU.add, op1=ALU.mult).then_inc(gate_ready, 1)

            def score(g, n, kind):
                h, tiles = GROUPS[n]
                dve.wait_ge(scores_ready, 6 * g + n + 1)
                alone(dve)
                col = 0
                for t in tiles:
                    w = (t + 1) * P
                    if kind == "fox":
                        b = bias[:, h, 0:w]
                    elif kind == "chk":
                        b = bias[:, h, S - w:S]
                    else:
                        b = sel_bias[:, OFF[t]:OFF[t] + w]
                    ins = dve.tensor_tensor_reduce(probs[:, h, OFF[t]:OFF[t] + w], score_bank[n % 3][:, col:col + w],
                                                   b, -1.0, BIG, ALU.add, ALU.min,
                                                   neg_max[:, 4 * h + t:4 * h + t + 1])
                    col += w
                ins.then_inc(scored, 1)

            def inverse(g, h):
                dve.wait_ge(exp_ready, 8 * g + 6 + 2 * h)
                dve.reciprocal(row_inv[:, 4 * h:4 * h + 4], row_sum[:, 4 * h:4 * h + 4]).then_inc(inv_ready, 1)

            def search(rounds):
                for _ in range(rounds):
                    found = []
                    for t in (1, 2, 3):
                        row = work[:, W_OFF[t]:W_OFF[t] + (t + 1) * P]
                        found.append(st.mark(dve.max(best8[:, t - 1, :], row)))
                    for t in (1, 2, 3):
                        row = work[:, W_OFF[t]:W_OFF[t] + (t + 1) * P]
                        st.wait(found[t - 1])
                        alone(dve)
                        last = st.mark(dve.match_replace(row, best8[:, t - 1, :], row, TAKEN))
                    st.wait(last)
                    alone(dve)

            def mix_pair(g):
                dve.wait_ge(pv_done, 2 * g + 2)
                wait_past(dve, mix_lo_ready, g)
                dve.wait_ge(gate_ready, g + 1)
                dve.scalar_tensor_tensor(out=mix[:, :], in0=pv_bank[:, :], scalar=0.5, in1=gate,
                                         op0=ALU.mult, op1=ALU.mult).then_inc(mixed, 1)

            def mix_low(g, pair):
                dve.wait_ge(mix_hi_ready, g + 1)
                dve.tensor_tensor(mix_lo[:, pair, :], mix[:, :], mix_hi[:, pair, :].bitcast(F32), ALU.subtract)\
                    .then_inc(mix_lo_ready, 1)

            def project(a, r, rotary):
                split_lo(r + 1, 0)
                q_low(a, r, rotary)
                split_lo(r + 1, 1)
                k_low(a, r, rotary)
                split_lo(r + 1, 2)
                gate_make(a)
                split_lo(r + 1, 3)

            def body(g, pair, kind, nxt, shift=0):
                r = g + 2 + shift
                if kind == "fox":
                    dve.wait_ge(bias_landed, 16 * g + 16)
                if kind == "chk":
                    dve.wait_ge(bias_landed, 64 + 16 * (g - 8) + 16)
                wait_past(dve, pt_ready, 6 * g)
                for n in range(3):
                    score(g, n, kind)
                if nxt:
                    split_lo(r + 1, 0)
                for n in range(3, 6):
                    score(g, n, kind)
                inverse(g, 0)
                inverse(g, 1)
                if nxt:
                    q_low(g + 1, r, nxt == "dsa")
                    split_lo(r + 1, 1)
                    k_low(g + 1, r, nxt == "dsa")
                if kind == "fox":
                    search(2)
                if nxt:
                    split_lo(r + 1, 2)
                if kind == "fox":
                    search(2)
                if nxt:
                    split_lo(r + 1, 3)
                mix_pair(g)
                if nxt:
                    gate_make(g + 1)
                mix_low(g, pair)

            x_scale(0, 0)
            x_scale(0, 1)
            dve.wait_ge(ws_hi_ready, 1)
            dve.tensor_tensor(ws_lo[:, :, :], ws_raw, ws_hi[:, :, :].bitcast(F32), ALU.subtract)\
                .then_inc(ws_lo_ready, 1)
            h_low(0, 0)
            x_scale(0, 2)
            h_low(0, 1)
            x_scale(0, 3)
            split_lo(0, 0)
            h_low(0, 2)
            h_low(0, 3)
            for j in range(1, 4):
                split_lo(0, j)

            dve.wait_ge(consts_landed, 16 * 8)
            dve.wait_ge(sumsq_ready, NT)
            st.done(dve.tensor_copy(angle, pos_i))
            st.done(dve.tensor_scalar(angle, angle, rope_c[:, 0:1], None, ALU.mult))
            for quarter, target, sign in ((0.0, rope_b[:, :], 0), (0.25, rope_a[:, :], 1)):
                st.done(dve.tensor_scalar(turns, angle, 1.0 / TWO_PI, quarter, ALU.mult, ALU.add))
                st.done(dve.tensor_scalar(turns, turns, ROUND_MAGIC, -ROUND_MAGIC, ALU.add, ALU.add))
                st.done(dve.scalar_tensor_tensor(out=target, in0=turns, scalar=-PI_HI, in1=angle,
                                                 op0=ALU.mult, op1=ALU.add))
                st.done(dve.scalar_tensor_tensor(out=target, in0=turns, scalar=-PI_MID, in1=target,
                                                 op0=ALU.mult, op1=ALU.add))
                st.done(dve.scalar_tensor_tensor(out=target, in0=turns, scalar=-PI_LO, in1=target,
                                                 op0=ALU.mult, op1=ALU.add))
                if sign:
                    st.done(dve.tensor_scalar(target, target, TWO_PI / 4, None, ALU.add))
                dve.tensor_scalar(target, target, PI_MAX, -PI_MAX, ALU.min, ALU.max).then_inc(angle_ready, 1)
            dve.wait_ge(sine_ready, 2)
            dve.tensor_scalar(sin_t[:, :], sin_t[:, :], rope_c[:, 1:2], None, ALU.mult)
            st.done(dve.tensor_scalar(cos_t[:, :], cos_t[:, :], rope_c[:, 2:3], rope_c[:, 3:4], ALU.mult, ALU.add))

            rows = slice(F_ROW, F_ROW + 8)
            dve.wait_ge(small_ready, 1)
            dve.tensor_scalar(fz, small[rows, :], b_f[rows, 0:1], None, ALU.add).then_inc(fz_ready, 1)
            st.done(dve.memset(ones8, 1.0))
            left = EXT - TAB
            dve.tensor_copy(ext[:, left:EXT], tab[:, ::-1])
            dve.tensor_copy(ext[:, 0:left], tab[:, TAB - 1:TAB].to_broadcast([16, left])).then_inc(ext_ready, 1)

            dve.wait_ge(small_t_ready, 1)
            st.done(dve.tensor_copy(small_tok[:, :, :], bank[1][:, 0:NT * P]
                                    .rearrange("p (t c) -> p t c", t=NT)[:, :, 0:SMALL]))
            iw = small_tok[:, :, IW_ROW:IW_ROW + 8]
            st.done(dve.tensor_scalar(iw, iw, IDX_SCALE, None, ALU.mult))
            ik = small_tok[:, :, 0:HD]
            stat = [ik_stat[:, n, :] for n in range(4)]

            def spread(col):
                return ik_stat[:, col, :].rearrange("p (t o) -> p t o", o=1).to_broadcast([P, NT, HD])

            st.done(dve.tensor_reduce(stat[0], ik, AX.X, ALU.add))
            st.done(dve.tensor_scalar(stat[0], stat[0], 1.0 / HD, None, ALU.mult))
            st.done(dve.tensor_tensor(ik_c, ik, spread(0), ALU.subtract))
            st.done(dve.tensor_tensor(ik_sq, ik_c, ik_c, ALU.mult))
            st.done(dve.tensor_reduce(stat[1], ik_sq, AX.X, ALU.add))
            dve.tensor_scalar(stat[1], stat[1], 1.0 / HD, EPS, ALU.mult, ALU.add).then_inc(ik_var_ready, 1)
            dve.wait_ge(ik_rstd_ready, 1)
            dve.tensor_tensor(ik_dup[:, :, 0, :], ik_c, spread(2), ALU.mult)
            dve.tensor_tensor(ik_dup[:, :, 1, :], ik_c, spread(2), ALU.mult).then_inc(ik_dup_ready, 1)

            dve.wait_ge(fl_ready, 1)
            st.done(dve.tensor_scalar(fz, fz, 0.0, None, ALU.min))
            st.done(dve.tensor_tensor(fz, fa, fz, ALU.subtract))
            dve.tensor_tensor_scan(small[rows, :], ones8, fz, 0.0, ALU.mult, ALU.add).then_inc(neg_f_ready, 1)
            dve.wait_ge(neg_f_ready, 1)

            def idx_low(n, hi, lo, src, scale=1.0):
                rope(src, scale).then_inc(i_roped, 1)
                dve.wait_ge(i_roped, n + 1)
                dve.wait_ge(i_hi_ready, n + 1)
                dve.tensor_tensor(lo, rope_b[:, :], hi.bitcast(F32), ALU.subtract).then_inc(i_lo_ready, 1)
                dve.wait_ge(i_lo_ready, n + 1)

            for j in range(IDX_UNITS):
                dve.wait_ge(unit_used, j + 1)
                idx_low(j, iq_hi[:, j, :], iq_lo[:, j, :], proj_bank[j % 2][:, :])
                split_lo(1, j)
            dve.wait_ge(ik_t_ready, 1)
            st.done(dve.tensor_scalar(ik_gained, bank[2][:, :], ik_gb[:, 0:1], ik_gb[:, 1:2], ALU.mult, ALU.add))
            idx_low(4, ik_hi, ik_lo, ik_gained)

            def index_step(s):
                t, h = s % 3 + 1, s // 3
                w = (t + 1) * P
                row = work[:, W_OFF[t]:W_OFF[t] + w]
                weight = small_tok[:, t, IW_ROW + h:IW_ROW + h + 1]
                dve.wait_ge(relu_ready, s + 1)
                if h == 0:
                    dve.tensor_scalar(row, relu[:, s % 2, 0:w], weight, None, ALU.mult).then_inc(relu_used, 1)
                else:
                    dve.wait_ge(relu_used, s - 2)
                    dve.scalar_tensor_tensor(out=row, in0=relu[:, s % 2, 0:w], scalar=weight, in1=row,
                                             op0=ALU.mult, op1=ALU.add).then_inc(relu_used, 1)

            split_lo(2, 0)
            q_low(0, 1, False)
            for s in range(0, 8):
                index_step(s)
            split_lo(2, 1)
            k_low(0, 1, False)
            for s in range(8, 16):
                index_step(s)
            split_lo(2, 2)
            for s in range(16, 24):
                index_step(s)
            dve.wait_ge(relu_used, 24)
            for t in (1, 2, 3):
                end = W_OFF[t] + (t + 1) * P
                last = st.mark(dve.memset(work[0:CHUNK, end - CHUNK:end], NEG))
            gate_make(0)
            split_lo(2, 3)
            st.wait(last)

            per_search = 2 * 2 * 6
            body(0, 0, "fox", "fox")
            with st.loop(2, per_search) as i:
                body(i + 1, i + 1, "fox", "fox")
            body(3, 3, "fox", "dsa")
            for t in (1, 2, 3):
                w = (t + 1) * P
                last = st.mark(dve.tensor_scalar(sel_bias[:, OFF[t]:OFF[t] + w], work[:, W_OFF[t]:W_OFF[t] + w],
                                                 TAKEN, NEG, ALU.not_equal, ALU.mult))
            st.wait(last)
            dve.wait_ge(consts_ready, 1)
            with st.loop(3, 6) as i:
                body(i + 4, i + 4, "dsa", "dsa")
            body(7, 7, "dsa", None)

            def out_norms(layer, r, last):
                for j in range(4):
                    split_lo(r + 1, j)
                for j in range(4):
                    split_lo(r + 2, j)
                y_scale(layer, 0)
                y_scale(layer, 1)
                for j in range(4):
                    split_lo(r + 3, j)
                    if not last and j < 2:
                        x_scale(1, j)
                if not last:
                    h_low(1, 0)
                    h_low(1, 1)
                    for j in range(4):
                        split_lo(r + 4, j)
                y_scale(layer, 2)
                y_scale(layer, 3)
                if not last:
                    x_scale(1, 2)
                    x_scale(1, 3)
                    h_low(1, 2)
                    h_low(1, 3)

            out_norms(0, 9, False)
            project(8, 13, False)
            with st.loop(7, 0) as i:
                body(i + 8, i, "chk", "chk", 4)
            body(15, 7, "chk", None)
            out_norms(1, 21, True)

        @block.tensor
        def _(pe):
            def transpose_x(layer, t):
                pe.wait_ge(normed_ready, NT * layer + t + 1)
                if t >= 2:
                    pe.wait_ge(h_lo_ready, 2 * (NT * layer + t - 1))
                elif layer:
                    pe.wait_ge(y_read, t + 1)
                for half in range(2):
                    for k in range(4):
                        src = normed[:, t % 2, (4 * half + k) * P:(4 * half + k + 1) * P]
                        ins = pe.transpose(bank[2 * (t % 2) + half][:, k * P:(k + 1) * P], src, ident[:, :])
                    ins.then_inc(xt_ready, 1)

            def three_passes(dst, a_hi, a_lo, b_hi, b_lo, start, stop):
                pe.matmul(dst, a_hi, b_hi, start=start, stop=False)
                pe.matmul(dst, a_hi, b_lo, start=False, stop=False)
                return pe.matmul(dst, a_lo, b_hi, start=False, stop=stop)

            def unit(r, j, dst):
                pe.wait_ge(w_lo_ready, 4 * r + j + 1)
                for k in range(KT):
                    cols = slice(k * P, (k + 1) * P)
                    ins = three_passes(dst[:, :], w_hi[:, j, cols], w_lo[:, j, cols], h_hi[:, k, :], h_lo[:, k, :],
                                       k == 0, k == KT - 1)
                ins.then_inc(unit_used, 1)

            def unit_q(a, r):
                wait_past(pe, v_staged, a)
                unit(r, 0, proj_bank[0])

            def unit_k(a, r):
                wait_past(pe, gate_ready, a)
                unit(r, 1, proj_bank[1])

            def unit_v(a, r):
                pe.wait_ge(q_ready, a + 1)
                unit(r, 2, proj_bank[0])

            def unit_g(a, r):
                pe.wait_ge(k_ready, a + 1)
                unit(r, 3, proj_bank[1])

            def turn_v(a):
                pe.wait_ge(v_staged, a + 1)
                wait_past(pe, scored, 6 * a)
                for t in range(NT):
                    ins = pe.transpose(score_bank[2][:, t * P:(t + 1) * P], v_t[:, t * P:(t + 1) * P], ident[:, :])
                ins.then_inc(vt_ready, 1)

            def scores(g, n, kind):
                h, tiles = GROUPS[n]
                if n == 2:
                    pe.wait_ge(v_ready, g + 1)
                if n >= 3:
                    pe.wait_ge(scored, 6 * g + n - 2)
                rows, col = slice(HD * h, HD * h + HD), 0
                for t in tiles:
                    w = (t + 1) * P
                    dst, cols = score_bank[n % 3], slice(t * P, (t + 1) * P)
                    ins = three_passes(dst[:, col:col + w], q_hi[rows, cols], q_lo[rows, cols],
                                       k_hi[rows, 0:w], k_lo[rows, 0:w], True, kind == "dsa")
                    if kind != "dsa":
                        mask = causal_b if kind == "fox" else chunk_b
                        ins = pe.matmul(dst[:, col + w - P:col + w], ident_b[:, :], mask[:, :], start=False, stop=True)
                    col += w
                ins.then_inc(scores_ready, 1)

            def turn_probs(g, h):
                pe.wait_ge(probs_ready, 8 * g + 4 * h + 4)
                for n, keys in enumerate(([0], [1], [2, 3])):
                    m = 3 * h + n
                    wait_past(pe, pt_read, 6 * g + max(m - 1, 0))
                    col = 0
                    for k in keys:
                        for t in range(k, NT):
                            ins = pe.transpose(pt_bank[m % 2][:, col:col + P],
                                               probs[:, h, OFF[t] + k * P:OFF[t] + (k + 1) * P], ident[:, :])
                            col += P
                    ins.then_inc(pt_ready, 1)

            def weigh_v(g, h):
                pe.wait_ge(pt_read, 6 * g + 3 * h + 3)
                if h == 0:
                    wait_past(pe, mixed, g)
                    pe.wait_ge(v_ready, g + 1)
                rows = slice(HD * h, HD * h + HD)
                for k in range(NT):
                    ins = pe.matmul(pv_bank[rows, k * P:S], v[:, k, rows], probs_t[:, h, KOFF[k]:KOFF[k] + S - k * P],
                                    start=(k == 0), stop=(k == NT - 1))
                ins.then_inc(pv_done, 1)

            def body(g, kind, nxt, shift=0):
                r = g + 2 + shift
                pe.wait_ge(k_ready, g + 1)
                pe.wait_ge(q_ready, g + 1)
                for n in range(3):
                    scores(g, n, kind)
                if nxt:
                    unit_q(g + 1, r)
                for n in range(3, 6):
                    scores(g, n, kind)
                if nxt:
                    unit_k(g + 1, r)
                turn_probs(g, 0)
                if nxt:
                    unit_v(g + 1, r)
                weigh_v(g, 0)
                turn_probs(g, 1)
                if nxt:
                    unit_g(g + 1, r)
                weigh_v(g, 1)
                if nxt:
                    turn_v(g + 1)

            def out_unit(layer, r, k):
                half = (r - (9, 21)[layer]) // 2
                j = k % 4
                pe.wait_ge(w_lo_ready, 4 * r + j + 1)
                pe.wait_ge(mix_lo_ready, PAIRS * layer + k + 1)
                for t in (2 * half, 2 * half + 1):
                    toks = slice(t * P, (t + 1) * P)
                    for n in range(2):
                        cols = slice(n * S, (n + 1) * S)
                        ins = three_passes(bank[2 * t + n][:, :], mix_hi[:, k, toks], mix_lo[:, k, toks],
                                           w_hi[:, j, cols], w_lo[:, j, cols], k == 0, k == KT - 1)
                    if k == KT - 1 and t == 2 * half:
                        ins.then_inc(y_ready, 1)
                ins.then_inc(unit_used, 1)

            def out_projection(layer, r):
                pe.wait_ge(scored, 48 * (layer + 1))
                pe.wait_ge(v_staged, 8 * (layer + 1))
                for k in range(KT):
                    out_unit(layer, r + k // 4, k)
                pe.wait_ge(gate_ready, 8 * (layer + 1))
                pe.wait_ge(pt_read, 48 * (layer + 1))
                pe.wait_ge(mixed, 8 * (layer + 1))
                for k in range(KT):
                    out_unit(layer, r + 2 + k // 4, k)
                    if layer == 0 and k in (4, 5):
                        transpose_x(1, k - 4)
                if layer == 0:
                    transpose_x(1, 2)
                    transpose_x(1, 3)

            pe.wait_ge(consts_ready, 1)
            for t in range(NT):
                transpose_x(0, t)
            pe.wait_ge(ws_lo_ready, 1)
            pe.wait_ge(h_lo_ready, 2 * NT)
            for k in range(KT):
                ins = three_passes(bank[2][0:SMALL, :], ws_hi[:, k, :], ws_lo[:, k, :], h_hi[:, k, :], h_lo[:, k, :],
                                   k == 0, k == KT - 1)
            ins.then_inc(small_done, 1)
            unit(0, 0, proj_bank[0])
            pe.wait_ge(small_ready, 1)
            for t in range(NT):
                ins = pe.transpose(bank[1][:, t * P:t * P + SMALL], small[:, t * P:(t + 1) * P],
                                   ident[0:SMALL, 0:SMALL])
            ins.then_inc(small_t_ready, 1)
            unit(0, 1, proj_bank[1])
            for j in (2, 3):
                pe.wait_ge(i_lo_ready, j - 1)
                unit(0, j, proj_bank[j % 2])
            pe.wait_ge(ik_dup_ready, 1)
            for t in range(NT):
                ins = pe.transpose(bank[2][:, t * P:(t + 1) * P], ik_dup[:, t, :, :].rearrange("p c d -> p (c d)"),
                                   ident[:, :])
            ins.then_inc(ik_t_ready, 1)

            def index_scores(s):
                t, h = s % 3 + 1, s // 3
                if s >= 3:
                    pe.wait_ge(relu_ready, s - 2)
                rows, w, cols = slice(HD * (h % 2), HD * (h % 2) + HD), (t + 1) * P, slice(t * P, (t + 1) * P)
                three_passes(score_bank[s % 3][:, 0:w], iq_hi[rows, h // 2, cols], iq_lo[rows, h // 2, cols],
                             ik_hi[rows, 0:w], ik_lo[rows, 0:w], True, True).then_inc(idx_ready, 1)

            pe.wait_ge(i_lo_ready, 3)
            unit(1, 0, proj_bank[0])
            pe.wait_ge(i_lo_ready, 5)
            for s in range(0, 8):
                index_scores(s)
            unit(1, 1, proj_bank[1])
            for s in range(8, 16):
                index_scores(s)
            unit_v(0, 1)
            for s in range(16, 24):
                index_scores(s)
            unit_g(0, 1)
            pe.wait_ge(relu_ready, 24)
            turn_v(0)

            body(0, "fox", "fox")
            with pe.Fori(1, 3) as g:
                body(g, "fox", "fox")
            body(3, "fox", "dsa")
            with pe.Fori(4, 7) as g:
                body(g, "dsa", "dsa")
            body(7, "dsa", None)
            out_projection(0, 9)

            pe.wait_ge(h_lo_ready, 4 * NT)
            pe.wait_ge(y_read, NT)
            unit_q(8, 13)
            unit_k(8, 13)
            unit_v(8, 13)
            unit_g(8, 13)
            turn_v(8)
            with pe.Fori(8, 15) as g:
                body(g, "chk", "chk", 4)
            body(15, "chk", None)
            out_projection(1, 21)


def unit_columns(w, first, width, pair):
    cols = w[:, first + pair * P:first + pair * P + P]
    return cols.reshape(KT, P, P).transpose(1, 0, 2).reshape(P, KT * P)


def kernel(x, positions, pre_norm_g, post_norm_g, w_in_even, b_forget, idx_k_g, idx_k_b,
           w_out_even, w_in_odd, rel_bias, w_out_odd):
    import concourse.bacc as bacc
    from concourse.bass_utils import run_bass_kernel_spmd

    w0, w1 = np.asarray(w_in_even)[0], np.asarray(w_in_odd)[0]
    fq, fk, fv, ff, fg = 0, 512, 1024, 1536, 1544
    dq, dk, dv, iq, ik, iw, dg = 2056, 2568, 3080, 3592, 4104, 4168, 4176
    units = [unit_columns(w0, iq, P, j) for j in range(IDX_UNITS)]
    units += [unit_columns(w0, c, P, p) for p in range(4) for c in (fq, fk, fv, fg)]
    units += [unit_columns(w0, c, P, p) for p in range(4) for c in (dq, dk, dv, dg)]
    units += [np.asarray(w_out_even)[0, k * P:(k + 1) * P] for k in range(KT)]
    units += [unit_columns(w1, c, P, p) for p in range(PAIRS) for c in (0, D, 2 * D, 3 * D)]
    units += [np.asarray(w_out_odd)[0, k * P:(k + 1) * P] for k in range(KT)]
    small = np.concatenate([w0[:, ik:ik + HD], w0[:, ff:ff + 8], w0[:, iw:iw + 8]], axis=1)
    small = small.reshape(KT, P, SMALL).transpose(1, 0, 2).reshape(P, KT * SMALL)

    row = np.arange(P) % HD
    rotated = row < ROT
    freq = (THETA ** (-np.arange(0, ROT, 2) / ROT)).astype(np.float32)
    rope_consts = np.stack([np.where(rotated, freq[row % (ROT // 2)], 0),
                            np.where(rotated, np.where(row < ROT // 2, -1, 1), 0),
                            rotated, ~rotated], axis=1).astype(np.float32)

    arrays = {
        "x": np.ascontiguousarray(np.asarray(x)[0]),
        "positions": np.ascontiguousarray(np.asarray(positions)),
        "pre_g": np.ascontiguousarray(pre_norm_g),
        "post_g": np.ascontiguousarray(post_norm_g),
        "w_units": np.ascontiguousarray(np.stack(units)),
        "w_small": np.ascontiguousarray(small),
        "b_forget": np.ascontiguousarray(np.asarray(b_forget).reshape(8, 1)),
        "idx_g": np.ascontiguousarray(np.asarray(idx_k_g).reshape(HD, 1)),
        "idx_b": np.ascontiguousarray(np.asarray(idx_k_b).reshape(HD, 1)),
        "rel_bias": np.ascontiguousarray(np.asarray(rel_bias)[0]),
        "rope_consts": rope_consts,
    }
    nc = bacc.Bacc("TRN2", target_bir_lowering=False, num_devices=1)
    args = [nc.dram_tensor(n, a.shape, mybir.dt.from_np(a.dtype), kind="ExternalInput").ap()
            for n, a in arrays.items()]
    out = nc.dram_tensor("out", (S, D), F32, kind="ExternalOutput").ap()
    neg_f_dram = nc.dram_tensor("neg_f", (4, 2 * S), F32, kind="Internal").ap()
    ext_dram = nc.dram_tensor("ext", (PAIRS, 2 * P * EXT), F32, kind="Internal").ap()
    trunk_program(nc, *args, out, neg_f_dram, ext_dram)
    r = run_bass_kernel_spmd(nc, [arrays], core_ids=[0])
    return r.results[0]["out"].reshape(1, S, D)
```

```python
from contextlib import ExitStack, contextmanager

import numpy as np

import concourse.bass as bass
from concourse import mybir

F32 = mybir.dt.float32
F32R = mybir.dt.float32r
BF16 = mybir.dt.bfloat16
I32 = mybir.dt.int32
ALU = mybir.AluOpType
ACT = mybir.ActivationFunctionType
AX = mybir.AxisListType

P = 128
D = 1024
S = 512
KT = D // P
NT = S // P
HD = 64
ROT = HD // 4
PAIRS = 8
FOX_PAIRS = 4
IDX_UNITS = 4
IDX_HEADS = 8
SMALL = 80
F_ROW, IW_ROW = 64, 72
TOPK = min(256, S // 4)
ROUNDS = TOPK // 8
CHUNK = 64
REL = 128
TAB = 2 * REL + 1
EXT = 640
THETA = 500000.0
EPS = 1e-6
NEG = -1e30
TAKEN = -3e38
BIG = 3e38
SCALE = HD ** -0.5
IDX_SCALE = (IDX_HEADS * HD) ** -0.5
OFF = [0, 128, 384, 768]
PACK = 1280
W_OFF = [None, 0, 256, 640]
W_PACK = 1152
KOFF = [0, 512, 896, 1152]
TWO_PI = 2 * np.pi
PI_HI = 6.28125
PI_MID = float(np.float32(0.0019350051879882812))
PI_LO = float(np.float32(TWO_PI - PI_HI - PI_MID))
PI_MAX = 3.1415925
ROUND_MAGIC = 12582912.0
SWAP = [i + 8 if i < 8 else i - 8 if i < 16 else i for i in range(32)]

GROUPS = [(0, [3]), (1, [3]), (0, [2]), (1, [2]), (0, [1, 0]), (1, [1, 0])]


class Steps:

    def __init__(self, eng, sem):
        self.eng, self.sem, self.base, self.n = eng, sem, 0, 0

    def mark(self, ins):
        ins.then_inc(self.sem, 1)
        self.n += 1
        return self.base + self.n

    def wait(self, count):
        self.eng.wait_ge(self.sem, count)

    def done(self, ins):
        self.wait(self.mark(ins))

    @contextmanager
    def loop(self, count, per_turn):
        base, n = self.base, self.n
        with self.eng.Fori(0, count) as i:
            self.base, self.n = base + n + i * per_turn, 0
            yield i
            assert self.n == per_turn, self.n
        self.base, self.n = base + n + count * per_turn, 0


def wait_past(eng, semaphore, count):
    if not isinstance(count, int) or count > 0:
        eng.wait_ge(semaphore, count)


def alone(eng):
    eng.nop(nofuse=True)


def trunk_program(nc, x, positions, pre_g, post_g, w_units, w_small, b_forget, idx_g, idx_b,
                  rel_bias, rope_consts, out, neg_f_dram, ext_dram):
    with ExitStack() as ctx:
        def sb(name, shape, dt=F32):
            return ctx.enter_context(nc.sbuf_tensor(name, shape, dt))

        def sem(name):
            return ctx.enter_context(nc.semaphore(name))

        bank = [ctx.enter_context(nc.psum_tensor(f"bank{i}", [P, S], F32)) for i in range(8)]
        score_bank = bank[0:3]
        proj_bank = bank[3:5]
        pt_bank = bank[5:7]
        pv_bank = bank[7]
        tile_bank = [(bank[3], bank[4]), (bank[0], bank[1]), (bank[5], bank[6]), (bank[7], bank[2])]
        group_bank = [bank[0], bank[1], bank[2], bank[0], bank[1], bank[5]]

        xt = sb("xt", [P, NT, D])
        h_hi = sb("h_hi", [P, KT, S], F32R)
        h_lo = sb("h_lo", [P, KT, S], F32R)
        mix_hi = sb("mix_hi", [P, PAIRS, S], F32R)
        mix_lo = sb("mix_lo", [P, PAIRS, S], F32R)
        w_raw = sb("w_raw", [P, 4, D])
        w_hi = sb("w_hi", [P, 4, D], F32R)
        w_lo = sb("w_lo", [P, 4, D], F32R)
        q_hi = sb("q_hi", [P, S], F32R)
        q_lo = sb("q_lo", [P, S], F32R)
        k_hi = sb("k_hi", [P, S], F32R)
        k_lo = sb("k_lo", [P, S], F32R)
        v_t = sb("v_t", [P, S])
        v = sb("v", [P, NT, P])
        tanh_gate = sb("tanh_gate", [P, 2, S])
        tanh_g, gate = tanh_gate[:, 0, :], tanh_gate[:, 1, :]
        probs = sb("probs", [P, 2, PACK])
        probs_t = sb("probs_t", [P, 2, PACK])
        mix = sb("mix", [P, S])
        bias = sb("bias", [P, 2, S])
        neg_max = sb("neg_max", [P, 8])
        row_sum = sb("row_sum", [P, 8])
        row_inv = sb("row_inv", [P, 8])
        rope_a = sb("rope_a", [P, S])
        rope_b = sb("rope_b", [P, S])
        k_roped = sb("k_roped", [P, S])
        cos_t = sb("cos_t", [P, S])
        sin_t = sb("sin_t", [P, S])
        work = sb("work", [P, W_PACK])
        sel_bias = sb("sel_bias", [P, PACK])
        best8 = sb("best8", [P, 3, 8])
        ws_hi = sb("ws_hi", [P, KT, SMALL], F32R)
        ws_lo = sb("ws_lo", [P, KT, SMALL], F32R)
        small_tok = sb("small_tok", [P, NT, SMALL])
        ik_stat = sb("ik_stat", [P, 4, NT])
        ik_gb = sb("ik_gb", [P, 2])
        b_f = sb("b_f", [SMALL, 1])
        tab = sb("tab", [16, TAB])
        g_pre = sb("g_pre", [P, D])
        g_post = sb("g_post", [P, D])
        sum_sq = sb("sum_sq", [P, 2, 2, NT, 2])
        mean_sq = sb("mean_sq", [P, 2, 2, NT])
        rstd = sb("rstd", [P, 2, 2, NT])
        half_neg = sb("half_neg", [P, NT])
        ident = sb("ident", [P, P])
        ident_b = sb("ident_b", [P, P], BF16)
        causal_b = sb("causal_b", [P, P], BF16)
        chunk_b = sb("chunk_b", [P, P], BF16)
        rope_c = sb("rope_c", [P, 4])

        squares = tanh_gate[:, :, :].rearrange("p a s -> p (a s)")
        pos_i = v_t[:, :].bitcast(I32)
        small = mix[0:SMALL, :]
        ws_raw = bias[:, :, :].rearrange("p h s -> p (h s)")[:, 0:KT * SMALL].rearrange("p (k c) -> p k c", k=KT)
        normed = probs_t[:, :, 0:D]
        y_normed = probs[:, :, 0:D]
        relu = probs_t[:, :, 0:S]
        iq_hi, iq_lo = mix_hi[:, 0:4, :], mix_lo[:, 0:4, :]
        ik_hi, ik_lo = mix_hi[:, 4, :], mix_lo[:, 4, :]
        ik_c = probs[:, 0, 0:NT * HD].rearrange("p (t d) -> p t d", t=NT)
        ik_sq = probs[:, 0, 256:256 + NT * HD].rearrange("p (t d) -> p t d", t=NT)
        ik_dup = probs[:, 0, 512:512 + NT * P].rearrange("p (t c d) -> p t c d", t=NT, c=2)
        ik_gained = probs[:, 1, 0:S]
        angle, turns, reduced = squares[:, 0:S], squares[:, S:D], rope_a[:, :]
        fz, fa = (probs[F_ROW:F_ROW + 8, 1, a:a + S] for a in (512, 0))
        ones8 = rope_b[F_ROW:F_ROW + 8, :]
        ext = g_post[0:16, 0:EXT]

        x_landed = [sem(f"x_landed{t}") for t in range(NT)]
        raw_landed = [sem(f"raw_landed{j}") for j in range(4)]
        ws_landed = sem("ws_landed")
        consts_landed = sem("consts_landed")
        gpre_landed = sem("gpre_landed")
        gpost_landed = sem("gpost_landed")
        bias_landed = sem("bias_landed")
        neg_f_stored = sem("neg_f_stored")
        ext_stored = sem("ext_stored")
        out_stored = sem("out_stored")
        consts_ready = sem("consts_ready")
        sumsq_ready = sem("sumsq_ready")
        rstd_ready = sem("rstd_ready")
        normed_ready = sem("normed_ready")
        xt_ready = sem("xt_ready")
        h_hi_ready = sem("h_hi_ready")
        h_lo_ready = sem("h_lo_ready")
        y_ready = sem("y_ready")
        ysq_ready = sem("ysq_ready")
        yrstd_ready = sem("yrstd_ready")
        y_read = sem("y_read")
        x_added = sem("x_added")
        w_hi_ready = sem("w_hi_ready")
        w_lo_ready = sem("w_lo_ready")
        unit_used = sem("unit_used")
        ws_hi_ready = sem("ws_hi_ready")
        ws_lo_ready = sem("ws_lo_ready")
        q_hi_ready = sem("q_hi_ready")
        q_ready = sem("q_ready")
        k_hi_ready = sem("k_hi_ready")
        k_ready = sem("k_ready")
        roped = sem("roped")
        v_staged = sem("v_staged")
        vt_ready = sem("vt_ready")
        v_ready = sem("v_ready")
        tanh_ready = sem("tanh_ready")
        gate_ready = sem("gate_ready")
        scores_ready = sem("scores_ready")
        scored = sem("scored")
        exp_ready = sem("exp_ready")
        inv_ready = sem("inv_ready")
        probs_ready = sem("probs_ready")
        pt_ready = sem("pt_ready")
        pt_read = sem("pt_read")
        pv_done = sem("pv_done")
        mixed = sem("mixed")
        mix_hi_ready = sem("mix_hi_ready")
        mix_lo_ready = sem("mix_lo_ready")
        small_done = sem("small_done")
        small_ready = sem("small_ready")
        small_t_ready = sem("small_t_ready")
        ik_var_ready = sem("ik_var_ready")
        ik_rstd_ready = sem("ik_rstd_ready")
        ik_dup_ready = sem("ik_dup_ready")
        ik_t_ready = sem("ik_t_ready")
        iq_done = sem("iq_done")
        i_roped = sem("i_roped")
        i_hi_ready = sem("i_hi_ready")
        i_lo_ready = sem("i_lo_ready")
        idx_ready = sem("idx_ready")
        relu_ready = sem("relu_ready")
        relu_used = sem("relu_used")
        angle_ready = sem("angle_ready")
        sine_ready = sem("sine_ready")
        fz_ready = sem("fz_ready")
        fl_ready = sem("fl_ready")
        neg_f_ready = sem("neg_f_ready")
        ext_ready = sem("ext_ready")
        dve_steps = sem("dve_steps")
        act_steps = sem("act_steps")
        pool_steps = sem("pool_steps")

        def turn_bank(g, h, n):
            if n < 2:
                return pt_bank[n]
            return score_bank[h] if not isinstance(g, int) or g not in (7, 15) else score_bank[2]

        block = ctx.enter_context(nc.Block())

        @block.sync
        def _(sp):
            sp.dma_start(ws_raw, w_small.rearrange("p (k c) -> p k c", k=KT)).then_inc(ws_landed, 16)
            for j in range(4):
                sp.dma_start(w_raw[:, j, :], w_units[j]).then_inc(raw_landed[j], 16)

            def load_round(r, first):
                for j in range(4):
                    sp.wait_ge(w_lo_ready, 4 * (r - 1) + j + 1)
                    sp.dma_start(w_raw[:, j, :], w_units[first + j]).then_inc(raw_landed[j], 16)

            with sp.Fori(0, 10) as i:
                load_round(i + 1, 4 * i + 4)
            with sp.Fori(0, 12) as i:
                load_round(i + 11, 4 * i + 36)
            with sp.Fori(0, 2) as i:
                load_round(i + 23, 4 * i + 76)
            for t in range(NT):
                sp.wait_ge(x_added, NT + t + 1)
                sp.dma_start(out[t * P:(t + 1) * P, :], xt[:, t, :]).then_inc(out_stored, 16)
            sp.wait_ge(out_stored, 16 * NT)

        @block.gpsimd
        def _(pool):
            st = Steps(pool, pool_steps)
            pool.dma_start(g_pre[:, :], pre_g[0:1, :].partition_broadcast(P)).then_inc(gpre_landed, 16)
            pool.memset(half_neg[:, :], -0.5)
            pool.memset(sel_bias[:, 0:P], 0.0)
            pool.memset(ident[:, :], 0.0)
            pool.memset(causal_b[:, :], 0.0)
            st.done(pool.memset(chunk_b[:, :], 0.0))
            st.done(pool.affine_select(out=ident[:, :], in_=ident[:, :], compare_op=ALU.not_equal, fill=1.0,
                                       base=0, pattern=[[-1, P]], channel_multiplier=1))
            pool.affine_select(out=causal_b[:, :], in_=causal_b[:, :], compare_op=ALU.is_ge, fill=NEG,
                               base=0, pattern=[[-1, P]], channel_multiplier=1)
            pool.memset(chunk_b[0:CHUNK, CHUNK:P], NEG)
            pool.memset(sel_bias[0:CHUNK, CHUNK:P], NEG)
            pool.tensor_copy(ident_b[:, :], ident[:, :]).then_inc(consts_ready, 1)
            pool.dma_start(rope_c[:, :], rope_consts).then_inc(consts_landed, 16)
            pool.dma_start(pos_i, positions.partition_broadcast(P)).then_inc(consts_landed, 16)
            for half in range(2):
                for col, src in ((0, idx_g), (1, idx_b)):
                    pool.dma_start(ik_gb[HD * half:HD * half + HD, col:col + 1], src).then_inc(consts_landed, 16)
            pool.dma_start(b_f[F_ROW:F_ROW + 8, :], b_forget).then_inc(consts_landed, 16)
            pool.dma_start(tab[:, :], rel_bias).then_inc(consts_landed, 16)

            def x_rstd(layer, t):
                pool.wait_ge(sumsq_ready, NT * layer + t + 1)
                st.done(pool.tensor_scalar(mean_sq[:, layer, 0, t:t + 1], sum_sq[:, layer, 0, t, 0:1],
                                           1.0 / D, EPS, ALU.mult, ALU.add))
                pool.tensor_tensor(rstd[:, layer, 0, t:t + 1], mean_sq[:, layer, 0, t:t + 1],
                                   half_neg[:, 0:1], ALU.pow).then_inc(rstd_ready, 1)

            def y_rstd(layer, t):
                pool.wait_ge(ysq_ready, NT * layer + t + 1)
                both = sum_sq[:, layer, 1, t, :]
                st.done(pool.tensor_tensor(both[:, 0:1], both[:, 0:1], both[:, 1:2], ALU.add))
                st.done(pool.tensor_scalar(mean_sq[:, layer, 1, t:t + 1], both[:, 0:1],
                                           1.0 / D, EPS, ALU.mult, ALU.add))
                pool.tensor_tensor(rstd[:, layer, 1, t:t + 1], mean_sq[:, layer, 1, t:t + 1],
                                   half_neg[:, 0:1], ALU.pow).then_inc(yrstd_ready, 1)

            def normalise(g):
                for h in range(2):
                    pool.wait_ge(inv_ready, 2 * g + h + 1)
                    alone(pool)
                    for t in (3, 2, 1, 0):
                        seg = probs[:, h, OFF[t]:OFF[t] + (t + 1) * P]
                        pool.tensor_scalar(seg, seg, row_inv[:, 4 * h + t:4 * h + t + 1], 0.0,
                                           ALU.mult, ALU.add).then_inc(probs_ready, 1)

            def load_fox_bias(pair):
                src = neg_f_dram[pair].rearrange("(o n) -> o n", o=1).partition_broadcast(P)
                pool.dma_start(bias[:, :, :].rearrange("p h s -> p (h s)"), src).then_inc(bias_landed, 16)

            def load_chk_bias(pair):
                rows = ext_dram[pair].rearrange("(h n) -> h n", h=2)[:, P - 1:P - 1 + P * (EXT - 1)]
                src = rows.rearrange("h (p w) -> p h w", w=EXT - 1)[:, :, 0:S]
                pool.dma_start(bias[:, :, :], src).then_inc(bias_landed, 16)

            for t in range(NT):
                x_rstd(0, t)
            pool.wait_ge(normed_ready, NT)
            pool.dma_start(g_pre[:, :], pre_g[1:2, :].partition_broadcast(P)).then_inc(gpre_landed, 16)
            pool.wait_ge(ik_var_ready, 1)
            pool.tensor_tensor(ik_stat[:, 2, :], ik_stat[:, 1, :], half_neg[:, :], ALU.pow)\
                .then_inc(ik_rstd_ready, 1)
            pool.wait_ge(ext_ready, 1)
            pool.dma_start(ext_dram.rearrange("a (h p w) -> (a h) p w", h=2, p=P),
                           ext.rearrange("h (o w) -> h o w", o=1).to_broadcast([16, P, EXT]))\
                .then_inc(ext_stored, 16)
            pool.wait_ge(neg_f_ready, 1)
            pool.dma_start(neg_f_dram.rearrange("a (b s) -> (a b) s", b=2), small[F_ROW:F_ROW + 8, :])\
                .then_inc(neg_f_stored, 16)
            pool.wait_ge(neg_f_stored, 16)
            load_fox_bias(0)
            with pool.Fori(0, 3) as g:
                normalise(g)
                pool.wait_ge(scored, 6 * g + 6)
                load_fox_bias(g + 1)
            with pool.Fori(3, 8) as g:
                normalise(g)
            pool.wait_ge(ext_stored, 16)
            pool.dma_start(g_post[:, :], post_g[0:1, :].partition_broadcast(P)).then_inc(gpost_landed, 16)
            pool.wait_ge(scored, 24)
            load_chk_bias(0)
            for t in range(2):
                y_rstd(0, t)
            for t in range(2):
                x_rstd(1, t)
            for t in range(2, NT):
                y_rstd(0, t)
            pool.wait_ge(y_read, NT)
            pool.dma_start(g_post[:, :], post_g[1:2, :].partition_broadcast(P)).then_inc(gpost_landed, 16)
            for t in range(2, NT):
                x_rstd(1, t)
            with pool.Fori(0, 7) as i:
                normalise(i + 8)
                pool.wait_ge(scored, 6 * i + 54)
                load_chk_bias(i + 1)
            normalise(15)
            for t in range(NT):
                y_rstd(1, t)

        @block.scalar
        def _(act):
            st = Steps(act, act_steps)
            for t in range(NT):
                act.dma_start(xt[:, t, :], x[t * P:(t + 1) * P, :]).then_inc(x_landed[t], 16)

            def split_hi(r, j, first=False):
                act.wait_ge(raw_landed[j], 16 * r + 16)
                if not first:
                    act.wait_ge(unit_used, 4 * r + j - 3)
                act.activation(w_hi[:, j, :], w_raw[:, j, :], ACT.Copy).then_inc(w_hi_ready, 1)

            def x_square(layer, t):
                if layer == 0:
                    act.wait_ge(x_landed[t], 16)
                else:
                    act.wait_ge(x_added, t + 1)
                if layer or t:
                    act.wait_ge(sumsq_ready, NT * layer + t)
                if layer:
                    act.wait_ge(ysq_ready, 2 if t < 2 else 4)
                act.activation(squares[:, :], xt[:, t, :], ACT.Square,
                               accum_out=sum_sq[:, layer, 0, t, 0:1]).then_inc(sumsq_ready, 1)

            def h_high(layer, t):
                for half in range(2):
                    n = 2 * (NT * layer + t) + half
                    act.wait_ge(xt_ready, n + 1)
                    act.activation(h_hi[:, 4 * half:4 * half + 4, t * P:(t + 1) * P],
                                   tile_bank[t][half][:, :].rearrange("p (k s) -> p k s", k=4),
                                   ACT.Copy).then_inc(h_hi_ready, 1)

            def y_square(layer, t):
                if t % 2 == 0:
                    act.wait_ge(y_ready, 2 * layer + t // 2 + 1)
                else:
                    act.wait_ge(unit_used, 4 * ((9, 21)[layer] + t) + 4)
                if layer or t:
                    act.wait_ge(ysq_ready, NT * layer + t)
                if t in (0, 2):
                    act.wait_ge(sumsq_ready, (NT, NT + 2, 2 * NT, 2 * NT)[2 * layer + t // 2])
                for half in range(2):
                    ins = act.activation(squares[:, half * S:(half + 1) * S], tile_bank[t][half][:, :],
                                         ACT.Square, accum_out=sum_sq[:, layer, 1, t, half:half + 1])
                ins.then_inc(ysq_ready, 1)

            def exps(g, n):
                h, tiles = GROUPS[n]
                for t in tiles:
                    act.wait_ge(scored, 6 * g + n + 1)
                    seg = probs[:, h, OFF[t]:OFF[t] + (t + 1) * P]
                    act.activation(seg, seg, ACT.Exp, bias=neg_max[:, 4 * h + t:4 * h + t + 1], scale=-1.0,
                                   accum_out=row_sum[:, 4 * h + t:4 * h + t + 1]).then_inc(exp_ready, 1)

            def q_high(a, r, rope, src=proj_bank[0]):
                if not rope:
                    act.wait_ge(unit_used, 4 * r + 1)
                wait_past(act, scores_ready, 6 * a)
                if rope:
                    act.wait_ge(roped, 2 * (a - 4) + 1)
                    act.activation(q_hi[:, :], rope_b[:, :], ACT.Copy).then_inc(q_hi_ready, 1)
                else:
                    act.activation(q_hi[:, :], src[:, :], ACT.Copy, scale=SCALE).then_inc(q_hi_ready, 1)

            def k_high(a, r, rope, src=proj_bank[1]):
                if rope:
                    act.wait_ge(roped, 2 * (a - 4) + 2)
                    act.activation(k_hi[:, :], k_roped[:, :], ACT.Copy).then_inc(k_hi_ready, 1)
                else:
                    act.wait_ge(unit_used, 4 * r + 2)
                    act.activation(k_hi[:, :], src[:, :], ACT.Copy).then_inc(k_hi_ready, 1)

            def v_stage(a, r):
                act.wait_ge(unit_used, 4 * r + 3)
                wait_past(act, vt_ready, a)
                act.activation(v_t[:, :], proj_bank[0][:, :], ACT.Copy).then_inc(v_staged, 1)

            def gate_tanh(a, r):
                act.wait_ge(unit_used, 4 * r + 4)
                wait_past(act, gate_ready, a)
                act.activation(tanh_g, proj_bank[1][:, :], ACT.Tanh, scale=0.5).then_inc(tanh_ready, 1)

            def v_copy(a):
                act.wait_ge(vt_ready, a + 1)
                wait_past(act, pv_done, 2 * a)
                act.activation(v[:, :, :], score_bank[2][:, :].rearrange("p (t d) -> p t d", t=NT),
                               ACT.Copy).then_inc(v_ready, 1)

            def copy_probs_t(g, h):
                wait_past(act, pv_done, 2 * g)
                for n in range(3):
                    act.wait_ge(pt_ready, 6 * g + 3 * h + n + 1)
                    a, b = (0, 512, 896, 1280)[n:n + 2]
                    act.activation(probs_t[:, h, a:b], turn_bank(g, h, n)[:, 0:b - a], ACT.Copy)\
                        .then_inc(pt_read, 1)

            def mix_high(g, pair):
                act.wait_ge(mixed, g + 1)
                act.activation(mix_hi[:, pair, :], mix[:, :], ACT.Copy).then_inc(mix_hi_ready, 1)

            def project(a, r):
                split_hi(r + 1, 0)
                q_high(a, r, False, bank[0])
                split_hi(r + 1, 1)
                k_high(a, r, False, bank[1])
                v_stage(a, r)
                split_hi(r + 1, 2)
                gate_tanh(a, r)
                split_hi(r + 1, 3)

            def body(g, pair, nxt, shift=0):
                r = g + 2 + shift
                v_copy(g)
                for n in range(2):
                    exps(g, n)
                split_hi(r + 1, 0)
                for n in range(2, 6):
                    exps(g, n)
                q_high(g + 1, r, nxt == "dsa")
                split_hi(r + 1, 1)
                copy_probs_t(g, 0)
                k_high(g + 1, r, nxt == "dsa")
                v_stage(g + 1, r)
                split_hi(r + 1, 2)
                copy_probs_t(g, 1)
                gate_tanh(g + 1, r)
                split_hi(r + 1, 3)
                mix_high(g, pair)

            def last_body(g, pair, r):
                v_copy(g)
                for n in range(2):
                    exps(g, n)
                for n in range(2, 6):
                    exps(g, n)
                split_hi(r + 1, 0)
                split_hi(r + 1, 1)
                copy_probs_t(g, 0)
                split_hi(r + 1, 2)
                split_hi(r + 1, 3)
                copy_probs_t(g, 1)
                split_hi(r + 2, 0)
                split_hi(r + 2, 1)
                mix_high(g, pair)

            x_square(0, 0)
            x_square(0, 1)
            act.wait_ge(ws_landed, 16)
            act.activation(ws_hi[:, :, :], ws_raw, ACT.Copy).then_inc(ws_hi_ready, 1)
            x_square(0, 2)
            x_square(0, 3)
            split_hi(0, 0, first=True)
            h_high(0, 0)
            h_high(0, 1)
            split_hi(0, 1, first=True)
            h_high(0, 2)
            h_high(0, 3)
            split_hi(0, 2, first=True)
            split_hi(0, 3, first=True)
            act.wait_ge(angle_ready, 1)
            act.activation(sin_t[:, :], rope_b[:, :], ACT.Sin).then_inc(sine_ready, 1)
            act.wait_ge(angle_ready, 2)
            act.activation(cos_t[:, :], rope_a[:, :], ACT.Sin).then_inc(sine_ready, 1)
            act.wait_ge(small_done, 1)
            act.activation(small, bank[2][0:SMALL, :], ACT.Copy).then_inc(small_ready, 1)
            act.wait_ge(fz_ready, 1)
            st.done(act.activation(fa, fz, ACT.Abs))
            st.done(act.activation(fa, fa, ACT.Exp, scale=-1.0))
            act.activation(fa, fa, ACT.Ln, bias=1.0).then_inc(fl_ready, 1)
            for j in range(IDX_UNITS):
                split_hi(1, j)
                act.wait_ge(i_roped, j + 1)
                act.activation(iq_hi[:, j, :], rope_b[:, :], ACT.Copy).then_inc(i_hi_ready, 1)
            act.wait_ge(i_roped, IDX_UNITS + 1)
            act.activation(ik_hi, rope_b[:, :], ACT.Copy).then_inc(i_hi_ready, 1)

            def relu_step(s):
                t = s % 3 + 1
                act.wait_ge(idx_ready, s + 1)
                if s >= 2:
                    act.wait_ge(relu_used, s - 1)
                w = (t + 1) * P
                act.activation(relu[:, s % 2, 0:w], score_bank[s % 3][:, 0:w], ACT.Relu).then_inc(relu_ready, 1)

            split_hi(2, 0)
            q_high(0, 1, False)
            for s in range(0, 8):
                relu_step(s)
            split_hi(2, 1)
            k_high(0, 1, False)
            for s in range(8, 16):
                relu_step(s)
            v_stage(0, 1)
            split_hi(2, 2)
            for s in range(16, 24):
                relu_step(s)
            gate_tanh(0, 1)
            split_hi(2, 3)

            body(0, 0, "fox")
            with act.Fori(1, 3) as g:
                body(g, g, "fox")
            with act.Fori(3, 7) as g:
                body(g, g, "dsa")
            last_body(7, 7, 9)

            def out_norms(layer, r, last):
                for j in (2, 3):
                    split_hi(r + 2, j)
                y_square(layer, 0)
                y_square(layer, 1)
                split_hi(r + 3, 0)
                if not last:
                    x_square(1, 0)
                split_hi(r + 3, 1)
                if not last:
                    x_square(1, 1)
                split_hi(r + 3, 2)
                split_hi(r + 3, 3)
                if not last:
                    h_high(1, 0)
                    h_high(1, 1)
                    for j in range(3):
                        split_hi(r + 4, j)
                y_square(layer, 2)
                y_square(layer, 3)
                if not last:
                    split_hi(r + 4, 3)
                    x_square(1, 2)
                    x_square(1, 3)
                    h_high(1, 2)
                    h_high(1, 3)

            out_norms(0, 9, False)
            project(8, 13)
            with act.Fori(0, 7) as i:
                body(i + 8, i, "chk", 4)
            last_body(15, 7, 21)
            out_norms(1, 21, True)

        @block.vector
        def _(dve):
            st = Steps(dve, dve_steps)

            def split_lo(r, j):
                dve.wait_ge(w_hi_ready, 4 * r + j + 1)
                dve.tensor_tensor(w_lo[:, j, :], w_raw[:, j, :], w_hi[:, j, :].bitcast(F32), ALU.subtract)\
                    .then_inc(w_lo_ready, 1)

            def x_scale(layer, t):
                dve.wait_ge(rstd_ready, NT * layer + t + 1)
                if t == 0:
                    dve.wait_ge(gpre_landed, 16 * (layer + 1))
                if t >= 2:
                    dve.wait_ge(xt_ready, 2 * (NT * layer + t - 1))
                dve.scalar_tensor_tensor(out=normed[:, t % 2, :], in0=xt[:, t, :], scalar=rstd[:, layer, 0, t:t + 1],
                                         in1=g_pre[:, :], op0=ALU.mult, op1=ALU.mult).then_inc(normed_ready, 1)

            def h_low(layer, t):
                for half in range(2):
                    dve.wait_ge(h_hi_ready, 2 * (NT * layer + t) + half + 1)
                    ks = slice(4 * half, 4 * half + 4)
                    dve.tensor_tensor(h_lo[:, ks, t * P:(t + 1) * P],
                                      tile_bank[t][half][:, :].rearrange("p (k s) -> p k s", k=4),
                                      h_hi[:, ks, t * P:(t + 1) * P].bitcast(F32),
                                      ALU.subtract).then_inc(h_lo_ready, 1)

            def y_scale(layer, t):
                dve.wait_ge(yrstd_ready, NT * layer + t + 1)
                if t == 0:
                    dve.wait_ge(gpost_landed, 16 * (layer + 1))
                for half in range(2):
                    cols = slice(half * S, (half + 1) * S)
                    ins = dve.scalar_tensor_tensor(out=y_normed[:, t % 2, cols], in0=tile_bank[t][half][:, :],
                                                   scalar=rstd[:, layer, 1, t:t + 1], in1=g_post[:, cols],
                                                   op0=ALU.mult, op1=ALU.mult)
                ins.then_inc(y_read, 1)
                dve.wait_ge(y_read, NT * layer + t + 1)
                dve.tensor_tensor(xt[:, t, :], xt[:, t, :], y_normed[:, t % 2, :], ALU.add).then_inc(x_added, 1)

            def rope(src, scale, dst=rope_b):
                alone(dve)
                st.done(dve.stream_shuffle(rope_a[:, :], src, SWAP))
                a = st.mark(dve.scalar_tensor_tensor(out=rope_a[:, :], in0=rope_a[:, :], scalar=scale,
                                                     in1=sin_t[:, :], op0=ALU.mult, op1=ALU.mult))
                b = st.mark(dve.scalar_tensor_tensor(out=dst[:, :], in0=src, scalar=scale, in1=cos_t[:, :],
                                                     op0=ALU.mult, op1=ALU.mult))
                st.wait(b)
                return dve.tensor_tensor(dst[:, :], dst[:, :], rope_a[:, :], ALU.add)

            def q_low(a, r, rotary, src=proj_bank[0]):
                if rotary:
                    dve.wait_ge(unit_used, 4 * r + 1)
                    rope(proj_bank[0][:, :], SCALE).then_inc(roped, 1)
                    dve.wait_ge(roped, 2 * (a - 4) + 1)
                dve.wait_ge(q_hi_ready, a + 1)
                if rotary:
                    dve.tensor_tensor(q_lo[:, :], rope_b[:, :], q_hi[:, :].bitcast(F32), ALU.subtract)\
                        .then_inc(q_ready, 1)
                else:
                    dve.scalar_tensor_tensor(out=q_lo[:, :], in0=src[:, :], scalar=SCALE,
                                             in1=q_hi[:, :].bitcast(F32), op0=ALU.mult, op1=ALU.subtract)\
                        .then_inc(q_ready, 1)

            def k_low(a, r, rotary, src=proj_bank[1]):
                if rotary:
                    src = k_roped
                dve.wait_ge(k_hi_ready, a + 1)
                dve.tensor_tensor(k_lo[:, :], src[:, :], k_hi[:, :].bitcast(F32), ALU.subtract)\
                    .then_inc(k_ready, 1)

            def k_rope(a, r):
                dve.wait_ge(unit_used, 4 * r + 2)
                rope(proj_bank[1][:, :], 1.0, k_roped).then_inc(roped, 1)
                dve.wait_ge(roped, 2 * (a - 4) + 2)

            def gate_make(a):
                dve.wait_ge(tanh_ready, a + 1)
                wait_past(dve, mixed, a)
                dve.scalar_tensor_tensor(out=gate, in0=tanh_g, scalar=1.0, in1=proj_bank[1][:, :],
                                         op0=ALU.add, op1=ALU.mult).then_inc(gate_ready, 1)

            def score(g, n, kind):
                h, tiles = GROUPS[n]
                dve.wait_ge(scores_ready, 6 * g + n + 1)
                alone(dve)
                col = 0
                for t in tiles:
                    w = (t + 1) * P
                    if kind == "fox":
                        b = bias[:, h, 0:w]
                    elif kind == "chk":
                        b = bias[:, h, S - w:S]
                    else:
                        b = sel_bias[:, OFF[t]:OFF[t] + w]
                    ins = dve.tensor_tensor_reduce(probs[:, h, OFF[t]:OFF[t] + w], group_bank[n][:, col:col + w],
                                                   b, -1.0, BIG, ALU.add, ALU.min,
                                                   neg_max[:, 4 * h + t:4 * h + t + 1])
                    col += w
                ins.then_inc(scored, 1)

            def inverse(g, h):
                dve.wait_ge(exp_ready, 8 * g + 6 + 2 * h)
                dve.reciprocal(row_inv[:, 4 * h:4 * h + 4], row_sum[:, 4 * h:4 * h + 4]).then_inc(inv_ready, 1)

            def search(rounds):
                for _ in range(rounds):
                    found = []
                    for t in (1, 2, 3):
                        row = work[:, W_OFF[t]:W_OFF[t] + (t + 1) * P]
                        found.append(st.mark(dve.max(best8[:, t - 1, :], row)))
                    for t in (1, 2, 3):
                        row = work[:, W_OFF[t]:W_OFF[t] + (t + 1) * P]
                        st.wait(found[t - 1])
                        alone(dve)
                        last = st.mark(dve.match_replace(row, best8[:, t - 1, :], row, TAKEN))
                    st.wait(last)
                    alone(dve)

            def mix_pair(g):
                dve.wait_ge(pv_done, 2 * g + 2)
                wait_past(dve, mix_lo_ready, g)
                dve.wait_ge(gate_ready, g + 1)
                dve.scalar_tensor_tensor(out=mix[:, :], in0=pv_bank[:, :], scalar=0.5, in1=gate,
                                         op0=ALU.mult, op1=ALU.mult).then_inc(mixed, 1)

            def mix_low(g, pair):
                dve.wait_ge(mix_hi_ready, g + 1)
                dve.tensor_tensor(mix_lo[:, pair, :], mix[:, :], mix_hi[:, pair, :].bitcast(F32), ALU.subtract)\
                    .then_inc(mix_lo_ready, 1)

            def project(a, r):
                split_lo(r + 1, 0)
                q_low(a, r, False, bank[0])
                split_lo(r + 1, 1)
                k_low(a, r, False, bank[1])
                split_lo(r + 1, 2)
                gate_make(a)
                split_lo(r + 1, 3)

            def first_scores(g, kind):
                if kind == "fox":
                    dve.wait_ge(bias_landed, 16 * g + 16)
                if kind == "chk":
                    dve.wait_ge(bias_landed, 64 + 16 * (g - 8) + 16)
                wait_past(dve, pt_ready, 6 * g)
                score(g, 0, kind)
                score(g, 1, kind)

            def body(g, pair, kind, nxt, shift=0):
                r = g + 2 + shift
                first_scores(g, kind)
                for n in range(2, 6):
                    score(g, n, kind)
                split_lo(r + 1, 0)
                inverse(g, 0)
                inverse(g, 1)
                q_low(g + 1, r, nxt == "dsa")
                if nxt == "dsa":
                    k_rope(g + 1, r)
                split_lo(r + 1, 1)
                k_low(g + 1, r, nxt == "dsa")
                if kind == "fox":
                    search(2)
                split_lo(r + 1, 2)
                if kind == "fox":
                    search(2)
                split_lo(r + 1, 3)
                mix_pair(g)
                gate_make(g + 1)
                mix_low(g, pair)

            def last_body(g, pair, kind, r):
                first_scores(g, kind)
                for n in range(2, 6):
                    score(g, n, kind)
                inverse(g, 0)
                inverse(g, 1)
                for j in range(4):
                    split_lo(r + 1, j)
                split_lo(r + 2, 0)
                mix_pair(g)
                mix_low(g, pair)
                split_lo(r + 2, 1)

            x_scale(0, 0)
            x_scale(0, 1)
            dve.wait_ge(ws_hi_ready, 1)
            dve.tensor_tensor(ws_lo[:, :, :], ws_raw, ws_hi[:, :, :].bitcast(F32), ALU.subtract)\
                .then_inc(ws_lo_ready, 1)
            h_low(0, 0)
            x_scale(0, 2)
            h_low(0, 1)
            x_scale(0, 3)
            split_lo(0, 0)
            h_low(0, 2)
            h_low(0, 3)
            for j in range(1, 4):
                split_lo(0, j)

            dve.wait_ge(consts_landed, 16 * 8)
            dve.wait_ge(sumsq_ready, NT)
            st.done(dve.tensor_copy(angle, pos_i))
            st.done(dve.tensor_scalar(angle, angle, rope_c[:, 0:1], None, ALU.mult))
            for quarter, target, sign in ((0.0, rope_b[:, :], 0), (0.25, rope_a[:, :], 1)):
                st.done(dve.tensor_scalar(turns, angle, 1.0 / TWO_PI, quarter, ALU.mult, ALU.add))
                st.done(dve.tensor_scalar(turns, turns, ROUND_MAGIC, -ROUND_MAGIC, ALU.add, ALU.add))
                st.done(dve.scalar_tensor_tensor(out=target, in0=turns, scalar=-PI_HI, in1=angle,
                                                 op0=ALU.mult, op1=ALU.add))
                st.done(dve.scalar_tensor_tensor(out=target, in0=turns, scalar=-PI_MID, in1=target,
                                                 op0=ALU.mult, op1=ALU.add))
                st.done(dve.scalar_tensor_tensor(out=target, in0=turns, scalar=-PI_LO, in1=target,
                                                 op0=ALU.mult, op1=ALU.add))
                if sign:
                    st.done(dve.tensor_scalar(target, target, TWO_PI / 4, None, ALU.add))
                dve.tensor_scalar(target, target, PI_MAX, -PI_MAX, ALU.min, ALU.max).then_inc(angle_ready, 1)
            dve.wait_ge(sine_ready, 2)
            dve.tensor_scalar(sin_t[:, :], sin_t[:, :], rope_c[:, 1:2], None, ALU.mult)
            st.done(dve.tensor_scalar(cos_t[:, :], cos_t[:, :], rope_c[:, 2:3], rope_c[:, 3:4], ALU.mult, ALU.add))

            rows = slice(F_ROW, F_ROW + 8)
            dve.wait_ge(small_ready, 1)
            dve.tensor_scalar(fz, small[rows, :], b_f[rows, 0:1], None, ALU.add).then_inc(fz_ready, 1)
            st.done(dve.memset(ones8, 1.0))
            left = EXT - TAB
            dve.tensor_copy(ext[:, left:EXT], tab[:, ::-1])
            dve.tensor_copy(ext[:, 0:left], tab[:, TAB - 1:TAB].to_broadcast([16, left])).then_inc(ext_ready, 1)

            dve.wait_ge(small_t_ready, 1)
            st.done(dve.tensor_copy(small_tok[:, :, :], bank[1][:, 0:NT * P]
                                    .rearrange("p (t c) -> p t c", t=NT)[:, :, 0:SMALL]))
            iw = small_tok[:, :, IW_ROW:IW_ROW + 8]
            st.done(dve.tensor_scalar(iw, iw, IDX_SCALE, None, ALU.mult))
            ik = small_tok[:, :, 0:HD]
            stat = [ik_stat[:, n, :] for n in range(4)]

            def spread(col):
                return ik_stat[:, col, :].rearrange("p (t o) -> p t o", o=1).to_broadcast([P, NT, HD])

            st.done(dve.tensor_reduce(stat[0], ik, AX.X, ALU.add))
            st.done(dve.tensor_scalar(stat[0], stat[0], 1.0 / HD, None, ALU.mult))
            st.done(dve.tensor_tensor(ik_c, ik, spread(0), ALU.subtract))
            st.done(dve.tensor_tensor(ik_sq, ik_c, ik_c, ALU.mult))
            st.done(dve.tensor_reduce(stat[1], ik_sq, AX.X, ALU.add))
            dve.tensor_scalar(stat[1], stat[1], 1.0 / HD, EPS, ALU.mult, ALU.add).then_inc(ik_var_ready, 1)
            dve.wait_ge(ik_rstd_ready, 1)
            dve.tensor_tensor(ik_dup[:, :, 0, :], ik_c, spread(2), ALU.mult)
            dve.tensor_tensor(ik_dup[:, :, 1, :], ik_c, spread(2), ALU.mult).then_inc(ik_dup_ready, 1)

            dve.wait_ge(fl_ready, 1)
            st.done(dve.tensor_scalar(fz, fz, 0.0, None, ALU.min))
            st.done(dve.tensor_tensor(fz, fa, fz, ALU.subtract))
            dve.tensor_tensor_scan(small[rows, :], ones8, fz, 0.0, ALU.mult, ALU.add).then_inc(neg_f_ready, 1)
            dve.wait_ge(neg_f_ready, 1)

            def idx_low(n, hi, lo, src, scale=1.0):
                rope(src, scale).then_inc(i_roped, 1)
                dve.wait_ge(i_roped, n + 1)
                dve.wait_ge(i_hi_ready, n + 1)
                dve.tensor_tensor(lo, rope_b[:, :], hi.bitcast(F32), ALU.subtract).then_inc(i_lo_ready, 1)
                dve.wait_ge(i_lo_ready, n + 1)

            for j in range(IDX_UNITS):
                dve.wait_ge(unit_used, j + 1)
                idx_low(j, iq_hi[:, j, :], iq_lo[:, j, :], proj_bank[j % 2][:, :])
                split_lo(1, j)
            dve.wait_ge(ik_t_ready, 1)
            st.done(dve.tensor_scalar(ik_gained, bank[2][:, :], ik_gb[:, 0:1], ik_gb[:, 1:2], ALU.mult, ALU.add))
            idx_low(4, ik_hi, ik_lo, ik_gained)

            def index_step(s):
                t, h = s % 3 + 1, s // 3
                w = (t + 1) * P
                row = work[:, W_OFF[t]:W_OFF[t] + w]
                weight = small_tok[:, t, IW_ROW + h:IW_ROW + h + 1]
                dve.wait_ge(relu_ready, s + 1)
                if h == 0:
                    dve.tensor_scalar(row, relu[:, s % 2, 0:w], weight, None, ALU.mult).then_inc(relu_used, 1)
                else:
                    dve.wait_ge(relu_used, s - 2)
                    dve.scalar_tensor_tensor(out=row, in0=relu[:, s % 2, 0:w], scalar=weight, in1=row,
                                             op0=ALU.mult, op1=ALU.add).then_inc(relu_used, 1)

            split_lo(2, 0)
            q_low(0, 1, False)
            for s in range(0, 8):
                index_step(s)
            split_lo(2, 1)
            k_low(0, 1, False)
            for s in range(8, 16):
                index_step(s)
            split_lo(2, 2)
            for s in range(16, 24):
                index_step(s)
            dve.wait_ge(relu_used, 24)
            for t in (1, 2, 3):
                end = W_OFF[t] + (t + 1) * P
                last = st.mark(dve.memset(work[0:CHUNK, end - CHUNK:end], NEG))
            gate_make(0)
            split_lo(2, 3)
            st.wait(last)

            per_search = 2 * 2 * 6
            body(0, 0, "fox", "fox")
            with st.loop(2, per_search) as i:
                body(i + 1, i + 1, "fox", "fox")
            body(3, 3, "fox", "dsa")
            for t in (1, 2, 3):
                w = (t + 1) * P
                last = st.mark(dve.tensor_scalar(sel_bias[:, OFF[t]:OFF[t] + w], work[:, W_OFF[t]:W_OFF[t] + w],
                                                 TAKEN, NEG, ALU.not_equal, ALU.mult))
            st.wait(last)
            dve.wait_ge(consts_ready, 1)
            with st.loop(3, 6) as i:
                body(i + 4, i + 4, "dsa", "dsa")
            last_body(7, 7, "dsa", 9)

            def out_norms(layer, r, last):
                for j in (2, 3):
                    split_lo(r + 2, j)
                y_scale(layer, 0)
                y_scale(layer, 1)
                for j in range(4):
                    split_lo(r + 3, j)
                    if not last and j < 2:
                        x_scale(1, j)
                if not last:
                    h_low(1, 0)
                    h_low(1, 1)
                    for j in range(4):
                        split_lo(r + 4, j)
                y_scale(layer, 2)
                y_scale(layer, 3)
                if not last:
                    x_scale(1, 2)
                    x_scale(1, 3)
                    h_low(1, 2)
                    h_low(1, 3)

            out_norms(0, 9, False)
            project(8, 13)
            with st.loop(7, 0) as i:
                body(i + 8, i, "chk", "chk", 4)
            last_body(15, 7, "chk", 21)
            out_norms(1, 21, True)

        @block.tensor
        def _(pe):
            def transpose_x(layer, t):
                pe.wait_ge(normed_ready, NT * layer + t + 1)
                if layer:
                    pe.wait_ge(y_read, t + 1)
                for half in range(2):
                    for k in range(4):
                        src = normed[:, t % 2, (4 * half + k) * P:(4 * half + k + 1) * P]
                        ins = pe.transpose(tile_bank[t][half][:, k * P:(k + 1) * P], src, ident[:, :])
                    ins.then_inc(xt_ready, 1)

            def three_passes(dst, a_hi, a_lo, b_hi, b_lo, start, stop):
                pe.matmul(dst, a_hi, b_hi, start=start, stop=False)
                pe.matmul(dst, a_hi, b_lo, start=False, stop=False)
                return pe.matmul(dst, a_lo, b_hi, start=False, stop=stop)

            def unit(r, j, dst, first=0, last=S):
                pe.wait_ge(w_lo_ready, 4 * r + j + 1)
                toks = slice(first, last)
                for k in range(KT):
                    cols = slice(k * P, (k + 1) * P)
                    ins = three_passes(dst[:, toks], w_hi[:, j, cols], w_lo[:, j, cols], h_hi[:, k, toks],
                                       h_lo[:, k, toks], k == 0, k == KT - 1)
                if last == S:
                    ins.then_inc(unit_used, 1)

            def unit_q(a, r):
                wait_past(pe, v_staged, a)
                unit(r, 0, proj_bank[0])

            def unit_k(a, r):
                wait_past(pe, gate_ready, a)
                unit(r, 1, proj_bank[1])

            def unit_v(a, r, rotary=False):
                if rotary:
                    pe.wait_ge(roped, 2 * (a - 4) + 1)
                else:
                    pe.wait_ge(q_ready, a + 1)
                unit(r, 2, proj_bank[0])

            def unit_g(a, r, rotary=False):
                if rotary:
                    pe.wait_ge(roped, 2 * (a - 4) + 2)
                else:
                    pe.wait_ge(k_ready, a + 1)
                unit(r, 3, proj_bank[1])

            def turn_v(a):
                pe.wait_ge(v_staged, a + 1)
                wait_past(pe, scored, 6 * a)
                for t in range(NT):
                    ins = pe.transpose(score_bank[2][:, t * P:(t + 1) * P], v_t[:, t * P:(t + 1) * P], ident[:, :])
                ins.then_inc(vt_ready, 1)

            def scores(g, n, kind):
                h, tiles = GROUPS[n]
                if n == 2:
                    pe.wait_ge(v_ready, g + 1)
                if n in (3, 4):
                    pe.wait_ge(scored, 6 * g + n - 2)
                rows, col = slice(HD * h, HD * h + HD), 0
                for t in tiles:
                    w = (t + 1) * P
                    dst, cols = group_bank[n], slice(t * P, (t + 1) * P)
                    ins = three_passes(dst[:, col:col + w], q_hi[rows, cols], q_lo[rows, cols],
                                       k_hi[rows, 0:w], k_lo[rows, 0:w], True, kind == "dsa")
                    if kind != "dsa":
                        mask = causal_b if kind == "fox" else chunk_b
                        ins = pe.matmul(dst[:, col + w - P:col + w], ident_b[:, :], mask[:, :], start=False, stop=True)
                    col += w
                ins.then_inc(scores_ready, 1)

            def turn_probs(g, h):
                pe.wait_ge(probs_ready, 8 * g + 4 * h + 4)
                if h == 0:
                    pe.wait_ge(scored, 6 * g + 6)
                wait_past(pe, pt_read, 6 * g + 3 * h)
                for n, keys in enumerate(([0], [1], [2, 3])):
                    if n == 2 and turn_bank(g, h, n) is score_bank[h]:
                        pe.wait_ge(scored, 6 * g + 4 + h)
                    elif n == 2:
                        pe.wait_ge(scored, 6 * g + 3)
                    col = 0
                    for k in keys:
                        for t in range(k, NT):
                            ins = pe.transpose(turn_bank(g, h, n)[:, col:col + P],
                                               probs[:, h, OFF[t] + k * P:OFF[t] + (k + 1) * P], ident[:, :])
                            col += P
                    ins.then_inc(pt_ready, 1)

            def weigh_v(g, h):
                pe.wait_ge(pt_read, 6 * g + 3 * h + 3)
                if h == 0:
                    wait_past(pe, mixed, g)
                    pe.wait_ge(v_ready, g + 1)
                rows = slice(HD * h, HD * h + HD)
                for k in range(NT):
                    ins = pe.matmul(pv_bank[rows, k * P:S], v[:, k, rows], probs_t[:, h, KOFF[k]:KOFF[k] + S - k * P],
                                    start=(k == 0), stop=(k == NT - 1))
                ins.then_inc(pv_done, 1)

            def first_scores(g, kind):
                pe.wait_ge(k_ready, g + 1)
                pe.wait_ge(q_ready, g + 1)
                scores(g, 0, kind)
                scores(g, 1, kind)
                turn_v(g)

            def body(g, kind, nxt, shift=0):
                r = g + 2 + shift
                first_scores(g, kind)
                unit_q(g + 1, r)
                for n in range(2, 6):
                    scores(g, n, kind)
                unit_k(g + 1, r)
                turn_probs(g, 0)
                unit_v(g + 1, r, nxt == "dsa")
                weigh_v(g, 0)
                turn_probs(g, 1)
                unit_g(g + 1, r, nxt == "dsa")
                weigh_v(g, 1)

            def last_body(g, kind, layer, r):
                first_scores(g, kind)
                pe.wait_ge(gate_ready, g + 1)
                out_tile(layer, r, 0, 0)
                out_tile(layer, r, 1, 0)
                scores(g, 2, kind)
                scores(g, 3, kind)
                out_tile(layer, r, 2, 0)
                scores(g, 4, kind)
                scores(g, 5, kind)
                out_tile(layer, r, 3, 0)
                pe.wait_ge(scored, 6 * g + 5)
                out_tile(layer, r, 0, 1)
                out_tile(layer, r, 1, 1)
                turn_probs(g, 0)
                out_tile(layer, r, 2, 1)
                out_tile(layer, r, 3, 1)
                weigh_v(g, 0)
                turn_probs(g, 1)
                out_unit(layer, r + 1, 4)
                out_unit(layer, r + 1, 5)
                weigh_v(g, 1)
                out_unit(layer, r + 1, 6)
                out_unit(layer, r + 1, 7)

            def out_tile(layer, r, k, t):
                j, toks = k % 4, slice(t * P, (t + 1) * P)
                pe.wait_ge(w_lo_ready, 4 * r + j + 1)
                pe.wait_ge(mix_lo_ready, PAIRS * layer + k + 1)
                for n in range(2):
                    cols = slice(n * S, (n + 1) * S)
                    ins = three_passes(tile_bank[t][n][:, :], mix_hi[:, k, toks], mix_lo[:, k, toks],
                                       w_hi[:, j, cols], w_lo[:, j, cols], k == 0, k == KT - 1)
                if t % 2 == 1:
                    ins.then_inc(unit_used, 1)
                elif k == KT - 1:
                    ins.then_inc(y_ready, 1)

            def out_unit(layer, r, k):
                half = (r - (9, 21)[layer]) // 2
                out_tile(layer, r, k, 2 * half)
                out_tile(layer, r, k, 2 * half + 1)

            def second_half(layer, r):
                pe.wait_ge(pt_read, 48 * (layer + 1))
                pe.wait_ge(mixed, 8 * (layer + 1))
                for k in range(KT):
                    out_unit(layer, r + k // 4, k)
                    if layer == 0 and k in (4, 5):
                        transpose_x(1, k - 4)

            pe.wait_ge(consts_ready, 1)
            for t in range(NT):
                transpose_x(0, t)
            pe.wait_ge(ws_lo_ready, 1)
            pe.wait_ge(h_lo_ready, 2 * NT)
            for k in range(KT):
                ins = three_passes(bank[2][0:SMALL, :], ws_hi[:, k, :], ws_lo[:, k, :], h_hi[:, k, :], h_lo[:, k, :],
                                   k == 0, k == KT - 1)
            ins.then_inc(small_done, 1)
            unit(0, 0, proj_bank[0])
            pe.wait_ge(small_ready, 1)
            for t in range(NT):
                ins = pe.transpose(bank[1][:, t * P:t * P + SMALL], small[:, t * P:(t + 1) * P],
                                   ident[0:SMALL, 0:SMALL])
            ins.then_inc(small_t_ready, 1)
            unit(0, 1, proj_bank[1])
            for j in (2, 3):
                pe.wait_ge(i_lo_ready, j - 1)
                unit(0, j, proj_bank[j % 2])
            pe.wait_ge(ik_dup_ready, 1)
            for t in range(NT):
                ins = pe.transpose(bank[2][:, t * P:(t + 1) * P], ik_dup[:, t, :, :].rearrange("p c d -> p (c d)"),
                                   ident[:, :])
            ins.then_inc(ik_t_ready, 1)

            def index_scores(s):
                t, h = s % 3 + 1, s // 3
                if s >= 3:
                    pe.wait_ge(relu_ready, s - 2)
                rows, w, cols = slice(HD * (h % 2), HD * (h % 2) + HD), (t + 1) * P, slice(t * P, (t + 1) * P)
                three_passes(score_bank[s % 3][:, 0:w], iq_hi[rows, h // 2, cols], iq_lo[rows, h // 2, cols],
                             ik_hi[rows, 0:w], ik_lo[rows, 0:w], True, True).then_inc(idx_ready, 1)

            pe.wait_ge(i_lo_ready, 3)
            unit(1, 0, proj_bank[0])
            pe.wait_ge(i_lo_ready, 5)
            for s in range(0, 8):
                index_scores(s)
            unit(1, 1, proj_bank[1])
            for s in range(8, 16):
                index_scores(s)
            unit_v(0, 1)
            for s in range(16, 24):
                index_scores(s)
            unit_g(0, 1)
            pe.wait_ge(relu_ready, 24)

            body(0, "fox", "fox")
            with pe.Fori(1, 3) as g:
                body(g, "fox", "fox")
            body(3, "fox", "dsa")
            with pe.Fori(4, 7) as g:
                body(g, "dsa", "dsa")
            last_body(7, "dsa", 0, 9)
            second_half(0, 11)

            pe.wait_ge(h_lo_ready, 3 * NT)
            first_banks = (bank[0], bank[1], proj_bank[0], proj_bank[1])
            for j in range(4):
                unit(13, j, first_banks[j], 0, S // 2)
            transpose_x(1, 2)
            transpose_x(1, 3)
            pe.wait_ge(h_lo_ready, 4 * NT)
            for j in range(4):
                unit(13, j, first_banks[j], S // 2, S)
            with pe.Fori(8, 15) as g:
                body(g, "chk", "chk", 4)
            last_body(15, "chk", 1, 21)
            second_half(1, 23)


def unit_columns(w, first, width, pair):
    cols = w[:, first + pair * P:first + pair * P + P]
    return cols.reshape(KT, P, P).transpose(1, 0, 2).reshape(P, KT * P)


def kernel(x, positions, pre_norm_g, post_norm_g, w_in_even, b_forget, idx_k_g, idx_k_b,
           w_out_even, w_in_odd, rel_bias, w_out_odd):
    import concourse.bacc as bacc
    from concourse.bass_utils import run_bass_kernel_spmd

    w0, w1 = np.asarray(w_in_even)[0], np.asarray(w_in_odd)[0]
    fq, fk, fv, ff, fg = 0, 512, 1024, 1536, 1544
    dq, dk, dv, iq, ik, iw, dg = 2056, 2568, 3080, 3592, 4104, 4168, 4176
    units = [unit_columns(w0, iq, P, j) for j in range(IDX_UNITS)]
    units += [unit_columns(w0, c, P, p) for p in range(4) for c in (fq, fk, fv, fg)]
    units += [unit_columns(w0, c, P, p) for p in range(4) for c in (dq, dk, dv, dg)]
    units += [np.asarray(w_out_even)[0, k * P:(k + 1) * P] for k in range(KT)]
    units += [unit_columns(w1, c, P, p) for p in range(PAIRS) for c in (0, D, 2 * D, 3 * D)]
    units += [np.asarray(w_out_odd)[0, k * P:(k + 1) * P] for k in range(KT)]
    small = np.concatenate([w0[:, ik:ik + HD], w0[:, ff:ff + 8], w0[:, iw:iw + 8]], axis=1)
    small = small.reshape(KT, P, SMALL).transpose(1, 0, 2).reshape(P, KT * SMALL)

    row = np.arange(P) % HD
    rotated = row < ROT
    freq = (THETA ** (-np.arange(0, ROT, 2) / ROT)).astype(np.float32)
    rope_consts = np.stack([np.where(rotated, freq[row % (ROT // 2)], 0),
                            np.where(rotated, np.where(row < ROT // 2, -1, 1), 0),
                            rotated, ~rotated], axis=1).astype(np.float32)

    arrays = {
        "x": np.ascontiguousarray(np.asarray(x)[0]),
        "positions": np.ascontiguousarray(np.asarray(positions)),
        "pre_g": np.ascontiguousarray(pre_norm_g),
        "post_g": np.ascontiguousarray(post_norm_g),
        "w_units": np.ascontiguousarray(np.stack(units)),
        "w_small": np.ascontiguousarray(small),
        "b_forget": np.ascontiguousarray(np.asarray(b_forget).reshape(8, 1)),
        "idx_g": np.ascontiguousarray(np.asarray(idx_k_g).reshape(HD, 1)),
        "idx_b": np.ascontiguousarray(np.asarray(idx_k_b).reshape(HD, 1)),
        "rel_bias": np.ascontiguousarray(np.asarray(rel_bias)[0]),
        "rope_consts": rope_consts,
    }
    nc = bacc.Bacc("TRN2", target_bir_lowering=False, num_devices=1)
    args = [nc.dram_tensor(n, a.shape, mybir.dt.from_np(a.dtype), kind="ExternalInput").ap()
            for n, a in arrays.items()]
    out = nc.dram_tensor("out", (S, D), F32, kind="ExternalOutput").ap()
    neg_f_dram = nc.dram_tensor("neg_f", (4, 2 * S), F32, kind="Internal").ap()
    ext_dram = nc.dram_tensor("ext", (PAIRS, 2 * P * EXT), F32, kind="Internal").ap()
    trunk_program(nc, *args, out, neg_f_dram, ext_dram)
    r = run_bass_kernel_spmd(nc, [arrays], core_ids=[0])
    return r.results[0]["out"].reshape(1, S, D)
```

```python
from contextlib import ExitStack, contextmanager

import numpy as np

import concourse.bass as bass
from concourse import mybir

F32 = mybir.dt.float32
F32R = mybir.dt.float32r
BF16 = mybir.dt.bfloat16
I32 = mybir.dt.int32
ALU = mybir.AluOpType
ACT = mybir.ActivationFunctionType
AX = mybir.AxisListType

P = 128
D = 1024
S = 512
KT = D // P
NT = S // P
HD = 64
ROT = HD // 4
PAIRS = 8
FOX_PAIRS = 4
IDX_UNITS = 4
IDX_HEADS = 8
SMALL = 80
F_ROW, IW_ROW = 64, 72
TOPK = min(256, S // 4)
ROUNDS = TOPK // 8
CHUNK = 64
REL = 128
TAB = 2 * REL + 1
EXT = 640
THETA = 500000.0
EPS = 1e-6
NEG = -1e30
TAKEN = -3e38
BIG = 3e38
SCALE = HD ** -0.5
IDX_SCALE = (IDX_HEADS * HD) ** -0.5
OFF = [0, 128, 384, 768]
PACK = 1280
W_OFF = [None, 0, 256, 640]
W_PACK = 1152
KOFF = [0, 512, 896, 1152]
TWO_PI = 2 * np.pi
PI_HI = 6.28125
PI_MID = float(np.float32(0.0019350051879882812))
PI_LO = float(np.float32(TWO_PI - PI_HI - PI_MID))
PI_MAX = 3.1415925
ROUND_MAGIC = 12582912.0
SWAP = [i + 8 if i < 8 else i - 8 if i < 16 else i for i in range(32)]

GROUPS = [(0, [3]), (1, [3]), (0, [2]), (1, [2]), (0, [1, 0]), (1, [1, 0])]


class Steps:

    def __init__(self, eng, sem):
        self.eng, self.sem, self.base, self.n = eng, sem, 0, 0

    def mark(self, ins):
        ins.then_inc(self.sem, 1)
        self.n += 1
        return self.base + self.n

    def wait(self, count):
        self.eng.wait_ge(self.sem, count)

    def done(self, ins):
        self.wait(self.mark(ins))

    @contextmanager
    def loop(self, count, per_turn):
        base, n = self.base, self.n
        with self.eng.Fori(0, count) as i:
            self.base, self.n = base + n + i * per_turn, 0
            yield i
            assert self.n == per_turn, self.n
        self.base, self.n = base + n + count * per_turn, 0


def wait_past(eng, semaphore, count):
    if not isinstance(count, int) or count > 0:
        eng.wait_ge(semaphore, count)


def alone(eng):
    eng.nop(nofuse=True)


def trunk_program(nc, x, positions, pre_g, post_g, w_units, w_small, b_forget, idx_g, idx_b,
                  rel_bias, rope_consts, out, neg_f_dram, ext_dram):
    with ExitStack() as ctx:
        def sb(name, shape, dt=F32):
            return ctx.enter_context(nc.sbuf_tensor(name, shape, dt))

        def sem(name):
            return ctx.enter_context(nc.semaphore(name))

        bank = [ctx.enter_context(nc.psum_tensor(f"bank{i}", [P, S], F32)) for i in range(8)]
        score_bank = bank[0:3]
        proj_bank = bank[3:5]
        pt_bank = bank[5:7]
        pv_bank = bank[7]
        tile_bank = [(bank[3], bank[4]), (bank[0], bank[1]), (bank[5], bank[6]), (bank[7], bank[2])]
        group_bank = [bank[0], bank[1], bank[2], bank[0], bank[1], bank[5]]

        xt = sb("xt", [P, NT, D])
        h_hi = sb("h_hi", [P, KT, S], F32R)
        h_lo = sb("h_lo", [P, KT, S], F32R)
        mix_hi = sb("mix_hi", [P, PAIRS, S], F32R)
        mix_lo = sb("mix_lo", [P, PAIRS, S], F32R)
        w_raw = sb("w_raw", [P, 4, D])
        w_hi = sb("w_hi", [P, 4, D], F32R)
        w_lo = sb("w_lo", [P, 4, D], F32R)
        q_hi = sb("q_hi", [P, S], F32R)
        q_lo = sb("q_lo", [P, S], F32R)
        k_hi = sb("k_hi", [P, S], F32R)
        k_lo = sb("k_lo", [P, S], F32R)
        v_t = sb("v_t", [P, S])
        v = sb("v", [P, NT, P])
        tanh_gate = sb("tanh_gate", [P, 2, S])
        tanh_g, gate = tanh_gate[:, 0, :], tanh_gate[:, 1, :]
        probs = sb("probs", [P, 2, PACK])
        probs_t = sb("probs_t", [P, 2, PACK])
        mix = sb("mix", [P, S])
        bias = sb("bias", [P, 2, S])
        neg_max = sb("neg_max", [P, 8])
        row_sum = sb("row_sum", [P, 8])
        row_inv = sb("row_inv", [P, 8])
        rope_a = sb("rope_a", [P, S])
        rope_b = sb("rope_b", [P, S])
        k_roped = sb("k_roped", [P, S])
        roped_buf = [rope_b, k_roped]
        cos_t = sb("cos_t", [P, S])
        sin_t = sb("sin_t", [P, S])
        work = sb("work", [P, W_PACK])
        sel_bias = sb("sel_bias", [P, PACK])
        best8 = sb("best8", [P, 3, 8])
        ws_hi = sb("ws_hi", [P, KT, SMALL], F32R)
        ws_lo = sb("ws_lo", [P, KT, SMALL], F32R)
        small_tok = sb("small_tok", [P, NT, SMALL])
        ik_stat = sb("ik_stat", [P, 4, NT])
        ik_gb = sb("ik_gb", [P, 2])
        b_f = sb("b_f", [SMALL, 1])
        tab = sb("tab", [16, TAB])
        g_pre = sb("g_pre", [P, D])
        g_post = sb("g_post", [P, D])
        sum_sq = sb("sum_sq", [P, 2, 2, NT, 2])
        mean_sq = sb("mean_sq", [P, 2, 2, NT])
        rstd = sb("rstd", [P, 2, 2, NT])
        half_neg = sb("half_neg", [P, NT])
        ident = sb("ident", [P, P])
        ident_b = sb("ident_b", [P, P], BF16)
        causal_b = sb("causal_b", [P, P], BF16)
        rope_c = sb("rope_c", [P, 4])

        squares = tanh_gate[:, :, :].rearrange("p a s -> p (a s)")
        pos_i = v_t[:, :].bitcast(I32)
        small = mix[0:SMALL, :]
        ws_raw = bias[:, :, :].rearrange("p h s -> p (h s)")[:, 0:KT * SMALL].rearrange("p (k c) -> p k c", k=KT)
        normed = [[probs_t[:, 0, 0:D], probs_t[:, 1, 0:D], probs[:, 0, 0:D], probs[:, 1, 0:D]],
                  [probs_t[:, t % 2, 0:D] for t in range(NT)]]
        y_normed = probs[:, :, 0:D]
        relu = probs_t[:, :, 0:S]
        iq_hi, iq_lo = mix_hi[:, 0:4, :], mix_lo[:, 0:4, :]
        ik_hi, ik_lo = mix_hi[:, 4, :], mix_lo[:, 4, :]
        ik_c = probs[:, 0, 0:NT * HD].rearrange("p (t d) -> p t d", t=NT)
        ik_sq = probs[:, 0, 256:256 + NT * HD].rearrange("p (t d) -> p t d", t=NT)
        ik_dup = probs[:, 0, 512:512 + NT * P].rearrange("p (t c d) -> p t c d", t=NT, c=2)
        ik_gained = probs[:, 0, 0:S]
        angle, turns = cos_t[:, :], sin_t[:, :]
        fz, fa = (probs[F_ROW:F_ROW + 8, 1, a:a + S] for a in (512, 0))
        ones8 = bias[F_ROW:F_ROW + 8, 0, :]
        ext = g_post[0:16, 0:EXT]

        x_landed = [sem(f"x_landed{t}") for t in range(NT)]
        raw_landed = [sem(f"raw_landed{j}") for j in range(4)]
        ws_landed = sem("ws_landed")
        consts_landed = sem("consts_landed")
        rope_landed = sem("rope_landed")
        gpre_landed = [sem(f"gpre_landed{layer}") for layer in range(2)]
        gpost_landed = sem("gpost_landed")
        bias_landed = sem("bias_landed")
        bias_masked = sem("bias_masked")
        neg_f_stored = sem("neg_f_stored")
        ext_stored = sem("ext_stored")
        out_stored = sem("out_stored")
        consts_ready = sem("consts_ready")
        sumsq_ready = sem("sumsq_ready")
        rstd_ready = sem("rstd_ready")
        normed_ready = sem("normed_ready")
        xt_ready = sem("xt_ready")
        h_hi_ready = sem("h_hi_ready")
        h_lo_ready = sem("h_lo_ready")
        y_ready = sem("y_ready")
        ysq_ready = sem("ysq_ready")
        yrstd_ready = sem("yrstd_ready")
        y_read = sem("y_read")
        x_added = sem("x_added")
        w_hi_ready = sem("w_hi_ready")
        w_lo_ready = sem("w_lo_ready")
        unit_used = sem("unit_used")
        ws_hi_ready = sem("ws_hi_ready")
        ws_lo_ready = sem("ws_lo_ready")
        q_hi_ready = sem("q_hi_ready")
        q_ready = sem("q_ready")
        k_hi_ready = sem("k_hi_ready")
        k_ready = sem("k_ready")
        roped = sem("roped")
        v_staged = sem("v_staged")
        vt_ready = sem("vt_ready")
        v_ready = sem("v_ready")
        tanh_ready = sem("tanh_ready")
        gate_ready = sem("gate_ready")
        scores_ready = sem("scores_ready")
        scored = sem("scored")
        exp_ready = sem("exp_ready")
        inv_ready = sem("inv_ready")
        probs_ready = sem("probs_ready")
        pt_ready = sem("pt_ready")
        pt_read = sem("pt_read")
        pv_done = sem("pv_done")
        mixed = sem("mixed")
        mix_hi_ready = sem("mix_hi_ready")
        mix_lo_ready = sem("mix_lo_ready")
        small_done = sem("small_done")
        small_ready = sem("small_ready")
        small_t_ready = sem("small_t_ready")
        ik_var_ready = sem("ik_var_ready")
        ik_rstd_ready = sem("ik_rstd_ready")
        ik_dup_ready = sem("ik_dup_ready")
        ik_t_ready = sem("ik_t_ready")
        i_roped = sem("i_roped")
        i_hi_ready = sem("i_hi_ready")
        i_lo_ready = sem("i_lo_ready")
        idx_ready = sem("idx_ready")
        relu_ready = sem("relu_ready")
        relu_used = sem("relu_used")
        angle_ready = sem("angle_ready")
        sine_ready = sem("sine_ready")
        fz_ready = sem("fz_ready")
        fl_ready = sem("fl_ready")
        neg_f_ready = sem("neg_f_ready")
        ext_ready = sem("ext_ready")
        dve_steps = sem("dve_steps")
        act_steps = sem("act_steps")
        pool_steps = sem("pool_steps")

        def turn_bank(g, h, n):
            if n < 2:
                return pt_bank[n]
            return score_bank[h] if not isinstance(g, int) or g not in (7, 15) else score_bank[2]

        block = ctx.enter_context(nc.Block())

        @block.sync
        def _(sp):
            def load_x(t):
                sp.dma_start(xt[:, t, :], x[t * P:(t + 1) * P, :]).then_inc(x_landed[t], 16)

            load_x(0)
            sp.dma_start(g_pre[:, :], pre_g[0:1, :].partition_broadcast(P)).then_inc(gpre_landed[0], 16)
            for t in range(1, NT):
                load_x(t)
            sp.dma_start(ws_raw, w_small.rearrange("p (k c) -> p k c", k=KT)).then_inc(ws_landed, 16)
            sp.dma_start(rope_c[:, :], rope_consts).then_inc(rope_landed, 16)
            sp.dma_start(pos_i, positions.partition_broadcast(P)).then_inc(rope_landed, 16)
            sp.dma_start(w_raw[:, 0, :], w_units[0]).then_inc(raw_landed[0], 16)
            for half in range(2):
                for col, src in ((0, idx_g), (1, idx_b)):
                    sp.dma_start(ik_gb[HD * half:HD * half + HD, col:col + 1], src).then_inc(consts_landed, 16)
            sp.dma_start(b_f[F_ROW:F_ROW + 8, :], b_forget).then_inc(consts_landed, 16)
            sp.dma_start(tab[:, :], rel_bias).then_inc(consts_landed, 16)
            for j in range(1, 4):
                sp.dma_start(w_raw[:, j, :], w_units[j]).then_inc(raw_landed[j], 16)

            def load_round(r, first):
                for j in range(4):
                    sp.wait_ge(w_lo_ready, 4 * (r - 1) + j + 1)
                    sp.dma_start(w_raw[:, j, :], w_units[first + j]).then_inc(raw_landed[j], 16)

            with sp.Fori(0, 10) as i:
                load_round(i + 1, 4 * i + 4)
            with sp.Fori(0, 12) as i:
                load_round(i + 11, 4 * i + 36)
            with sp.Fori(0, 2) as i:
                load_round(i + 23, 4 * i + 76)
            for t in range(NT):
                sp.wait_ge(x_added, NT + t + 1)
                sp.dma_start(out[t * P:(t + 1) * P, :], xt[:, t, :]).then_inc(out_stored, 16)
            sp.wait_ge(out_stored, 16 * NT)

        @block.gpsimd
        def _(pool):
            st = Steps(pool, pool_steps)
            pool.memset(half_neg[:, :], -0.5)
            pool.memset(sel_bias[:, 0:P], 0.0)
            pool.memset(ident[:, :], 0.0)
            st.done(pool.memset(causal_b[:, :], 0.0))
            st.done(pool.affine_select(out=ident[:, :], in_=ident[:, :], compare_op=ALU.not_equal, fill=1.0,
                                       base=0, pattern=[[-1, P]], channel_multiplier=1))
            pool.affine_select(out=causal_b[:, :], in_=causal_b[:, :], compare_op=ALU.is_ge, fill=NEG,
                               base=0, pattern=[[-1, P]], channel_multiplier=1)
            pool.memset(sel_bias[0:CHUNK, CHUNK:P], NEG)
            pool.tensor_copy(ident_b[:, :], ident[:, :]).then_inc(consts_ready, 1)

            def x_rstd(layer, t):
                pool.wait_ge(sumsq_ready, NT * layer + t + 1)
                st.done(pool.tensor_scalar(mean_sq[:, layer, 0, t:t + 1], sum_sq[:, layer, 0, t, 0:1],
                                           1.0 / D, EPS, ALU.mult, ALU.add))
                pool.tensor_tensor(rstd[:, layer, 0, t:t + 1], mean_sq[:, layer, 0, t:t + 1],
                                   half_neg[:, 0:1], ALU.pow).then_inc(rstd_ready, 1)

            def y_rstd(layer, t):
                pool.wait_ge(ysq_ready, NT * layer + t + 1)
                both = sum_sq[:, layer, 1, t, :]
                st.done(pool.tensor_tensor(both[:, 0:1], both[:, 0:1], both[:, 1:2], ALU.add))
                st.done(pool.tensor_scalar(mean_sq[:, layer, 1, t:t + 1], both[:, 0:1],
                                           1.0 / D, EPS, ALU.mult, ALU.add))
                pool.tensor_tensor(rstd[:, layer, 1, t:t + 1], mean_sq[:, layer, 1, t:t + 1],
                                   half_neg[:, 0:1], ALU.pow).then_inc(yrstd_ready, 1)

            def split_lo(r, j):
                pool.wait_ge(w_lo_ready, 4 * r + j)
                pool.wait_ge(w_hi_ready, 4 * r + j + 1)
                pool.tensor_tensor(w_lo[:, j, :], w_raw[:, j, :], w_hi[:, j, :].bitcast(F32), ALU.subtract)\
                    .then_inc(w_lo_ready, 1)

            def normalise(g):
                for h in range(2):
                    pool.wait_ge(inv_ready, 2 * g + h + 1)
                    alone(pool)
                    for t in (3, 2, 1, 0):
                        seg = probs[:, h, OFF[t]:OFF[t] + (t + 1) * P]
                        pool.tensor_scalar(seg, seg, row_inv[:, 4 * h + t:4 * h + t + 1], 0.0,
                                           ALU.mult, ALU.add).then_inc(probs_ready, 1)

            def load_fox_bias(pair):
                src = neg_f_dram[pair].rearrange("(o n) -> o n", o=1).partition_broadcast(P)
                pool.dma_start(bias[:, :, :].rearrange("p h s -> p (h s)"), src).then_inc(bias_landed, 16)

            def load_chk_bias(pair):
                rows = ext_dram[pair].rearrange("(h n) -> h n", h=2)[:, P - 1:P - 1 + P * (EXT - 1)]
                src = rows.rearrange("h (p w) -> p h w", w=EXT - 1)[:, :, 0:S]
                pool.dma_start(bias[:, :, :], src).then_inc(bias_landed, 16)
                pool.wait_ge(bias_landed, 16 * (FOX_PAIRS + pair + 1))
                alone(pool)
                pool.memset(bias[0:CHUNK, :, S - CHUNK:S], NEG).then_inc(bias_masked, 1)

            for t in range(NT):
                x_rstd(0, t)
            pool.wait_ge(normed_ready, NT)
            pool.dma_start(g_pre[:, :], pre_g[1:2, :].partition_broadcast(P)).then_inc(gpre_landed[1], 16)
            pool.wait_ge(ik_var_ready, 1)
            pool.tensor_tensor(ik_stat[:, 2, :], ik_stat[:, 1, :], half_neg[:, :], ALU.pow)\
                .then_inc(ik_rstd_ready, 1)
            split_lo(1, 2)
            split_lo(1, 3)
            split_lo(2, 0)
            pool.wait_ge(neg_f_ready, 1)
            pool.dma_start(neg_f_dram.rearrange("a (b s) -> (a b) s", b=2), small[F_ROW:F_ROW + 8, :])\
                .then_inc(neg_f_stored, 16)
            pool.wait_ge(neg_f_stored, 16)
            load_fox_bias(0)
            split_lo(2, 1)
            pool.wait_ge(ext_ready, 1)
            pool.dma_start(ext_dram.rearrange("a (h p w) -> (a h) p w", h=2, p=P),
                           ext.rearrange("h (o w) -> h o w", o=1).to_broadcast([16, P, EXT]))\
                .then_inc(ext_stored, 16)
            with pool.Fori(0, 3) as g:
                split_lo(g + 3, 0)
                normalise(g)
                pool.wait_ge(scored, 6 * g + 6)
                load_fox_bias(g + 1)
            with pool.Fori(3, 7) as g:
                split_lo(g + 3, 0)
                normalise(g)
            normalise(7)
            pool.wait_ge(ext_stored, 16)
            pool.dma_start(g_post[:, :], post_g[0:1, :].partition_broadcast(P)).then_inc(gpost_landed, 16)
            pool.wait_ge(scored, 24)
            load_chk_bias(0)
            for t in range(2):
                y_rstd(0, t)
            for t in range(2):
                x_rstd(1, t)
            for t in range(2, NT):
                y_rstd(0, t)
            split_lo(13, 2)
            for t in range(2, NT):
                x_rstd(1, t)
            pool.wait_ge(y_read, NT)
            pool.dma_start(g_post[:, :], post_g[1:2, :].partition_broadcast(P)).then_inc(gpost_landed, 16)
            with pool.Fori(0, 7) as i:
                split_lo(i + 15, 0)
                normalise(i + 8)
                pool.wait_ge(scored, 6 * i + 54)
                load_chk_bias(i + 1)
            normalise(15)
            for t in range(NT):
                y_rstd(1, t)

        @block.scalar
        def _(act):
            st = Steps(act, act_steps)
            def split_hi(r, j, first=False):
                act.wait_ge(raw_landed[j], 16 * r + 16)
                if not first:
                    act.wait_ge(unit_used, 4 * r + j - 3)
                act.activation(w_hi[:, j, :], w_raw[:, j, :], ACT.Copy).then_inc(w_hi_ready, 1)

            def x_square(layer, t):
                if layer == 0:
                    act.wait_ge(x_landed[t], 16)
                else:
                    act.wait_ge(x_added, t + 1)
                if layer or t:
                    act.wait_ge(sumsq_ready, NT * layer + t)
                if layer:
                    act.wait_ge(ysq_ready, 2 if t < 2 else 4)
                act.activation(squares[:, :], xt[:, t, :], ACT.Square,
                               accum_out=sum_sq[:, layer, 0, t, 0:1]).then_inc(sumsq_ready, 1)

            def h_high(layer, t):
                for half in range(2):
                    n = 2 * (NT * layer + t) + half
                    act.wait_ge(xt_ready, n + 1)
                    act.activation(h_hi[:, 4 * half:4 * half + 4, t * P:(t + 1) * P],
                                   tile_bank[t][half][:, :].rearrange("p (k s) -> p k s", k=4),
                                   ACT.Copy).then_inc(h_hi_ready, 1)

            def y_square(layer, t):
                if t % 2 == 0:
                    act.wait_ge(y_ready, 2 * layer + t // 2 + 1)
                else:
                    act.wait_ge(unit_used, 4 * ((9, 21)[layer] + t) + 4)
                if layer or t:
                    act.wait_ge(ysq_ready, NT * layer + t)
                if t in (0, 2):
                    act.wait_ge(sumsq_ready, (NT, NT + 2, 2 * NT, 2 * NT)[2 * layer + t // 2])
                for half in range(2):
                    ins = act.activation(squares[:, half * S:(half + 1) * S], tile_bank[t][half][:, :],
                                         ACT.Square, accum_out=sum_sq[:, layer, 1, t, half:half + 1])
                ins.then_inc(ysq_ready, 1)

            def exps(g, n):
                h, tiles = GROUPS[n]
                for t in tiles:
                    act.wait_ge(scored, 6 * g + n + 1)
                    seg = probs[:, h, OFF[t]:OFF[t] + (t + 1) * P]
                    act.activation(seg, seg, ACT.Exp, bias=neg_max[:, 4 * h + t:4 * h + t + 1], scale=-1.0,
                                   accum_out=row_sum[:, 4 * h + t:4 * h + t + 1]).then_inc(exp_ready, 1)

            def q_high(a, r, rope, src=proj_bank[0]):
                if not rope:
                    act.wait_ge(unit_used, 4 * r + 1)
                wait_past(act, scores_ready, 6 * a)
                if rope:
                    act.wait_ge(roped, 2 * (a - 4) + 1)
                    act.activation(q_hi[:, :], rope_b[:, :], ACT.Copy).then_inc(q_hi_ready, 1)
                else:
                    act.activation(q_hi[:, :], src[:, :], ACT.Copy, scale=SCALE).then_inc(q_hi_ready, 1)

            def k_high(a, r, rope, src=proj_bank[1]):
                if rope:
                    act.wait_ge(roped, 2 * (a - 4) + 2)
                    act.activation(k_hi[:, :], k_roped[:, :], ACT.Copy).then_inc(k_hi_ready, 1)
                else:
                    act.wait_ge(unit_used, 4 * r + 2)
                    act.activation(k_hi[:, :], src[:, :], ACT.Copy).then_inc(k_hi_ready, 1)

            def v_stage(a, r):
                act.wait_ge(unit_used, 4 * r + 3)
                wait_past(act, vt_ready, a)
                act.activation(v_t[:, :], proj_bank[0][:, :], ACT.Copy).then_inc(v_staged, 1)

            def gate_tanh(a, r):
                act.wait_ge(unit_used, 4 * r + 4)
                wait_past(act, gate_ready, a)
                act.activation(tanh_g, proj_bank[1][:, :], ACT.Tanh, scale=0.5).then_inc(tanh_ready, 1)

            def v_copy(a):
                act.wait_ge(vt_ready, a + 1)
                wait_past(act, pv_done, 2 * a)
                act.activation(v[:, :, :], score_bank[2][:, :].rearrange("p (t d) -> p t d", t=NT),
                               ACT.Copy).then_inc(v_ready, 1)

            def copy_probs_t(g, h):
                wait_past(act, pv_done, 2 * g)
                for n in range(3):
                    act.wait_ge(pt_ready, 6 * g + 3 * h + n + 1)
                    a, b = (0, 512, 896, 1280)[n:n + 2]
                    act.activation(probs_t[:, h, a:b], turn_bank(g, h, n)[:, 0:b - a], ACT.Copy)\
                        .then_inc(pt_read, 1)

            def mix_high(g, pair):
                act.wait_ge(mixed, g + 1)
                act.activation(mix_hi[:, pair, :], mix[:, :], ACT.Copy).then_inc(mix_hi_ready, 1)

            def project(a, r):
                split_hi(r + 1, 0)
                q_high(a, r, False, bank[0])
                split_hi(r + 1, 1)
                k_high(a, r, False, bank[1])
                v_stage(a, r)
                split_hi(r + 1, 2)
                gate_tanh(a, r)
                split_hi(r + 1, 3)

            def body(g, pair, nxt, shift=0):
                r = g + 2 + shift
                v_copy(g)
                for n in range(2):
                    exps(g, n)
                split_hi(r + 1, 0)
                for n in range(2, 6):
                    exps(g, n)
                q_high(g + 1, r, nxt == "dsa")
                split_hi(r + 1, 1)
                copy_probs_t(g, 0)
                k_high(g + 1, r, nxt == "dsa")
                v_stage(g + 1, r)
                split_hi(r + 1, 2)
                copy_probs_t(g, 1)
                gate_tanh(g + 1, r)
                split_hi(r + 1, 3)
                mix_high(g, pair)

            def last_body(g, pair, r):
                v_copy(g)
                for n in range(2):
                    exps(g, n)
                for n in range(2, 6):
                    exps(g, n)
                split_hi(r + 1, 0)
                split_hi(r + 1, 1)
                copy_probs_t(g, 0)
                split_hi(r + 1, 2)
                split_hi(r + 1, 3)
                copy_probs_t(g, 1)
                split_hi(r + 2, 0)
                split_hi(r + 2, 1)
                mix_high(g, pair)

            act.wait_ge(consts_ready, 1)
            act.activation(row_sum[:, 0:NT], half_neg[:, :], ACT.Square)
            for t in range(NT):
                x_square(0, t)
            h_high(0, 0)
            act.wait_ge(ws_landed, 16)
            act.activation(ws_hi[:, :, :], ws_raw, ACT.Copy).then_inc(ws_hi_ready, 1)
            h_high(0, 1)
            h_high(0, 2)
            h_high(0, 3)
            for j in range(4):
                split_hi(0, j, first=True)
            act.wait_ge(small_done, 1)
            act.activation(small, bank[0][0:SMALL, :], ACT.Copy).then_inc(small_ready, 1)
            act.wait_ge(fz_ready, 1)
            st.done(act.activation(fa, fz, ACT.Abs))
            st.done(act.activation(fa, fa, ACT.Exp, scale=-1.0))
            act.activation(fa, fa, ACT.Ln, bias=1.0).then_inc(fl_ready, 1)
            q_high(0, 0, False)
            act.wait_ge(angle_ready, 2)
            act.activation(sin_t[:, :], rope_b[:, :], ACT.Sin).then_inc(sine_ready, 1)
            act.activation(cos_t[:, :], rope_a[:, :], ACT.Sin).then_inc(sine_ready, 1)

            def idx_high(n, hi):
                act.wait_ge(i_roped, n + 1)
                act.activation(hi, roped_buf[n % 2][:, :], ACT.Copy).then_inc(i_hi_ready, 1)

            def relu_steps(first, last):
                for s in range(first, last):
                    t = s % 3 + 1
                    act.wait_ge(idx_ready, s + 1)
                    if s >= 2:
                        act.wait_ge(relu_used, s - 1)
                    w = (t + 1) * P
                    act.activation(relu[:, s % 2, 0:w], score_bank[s % 3][:, 0:w], ACT.Relu)\
                        .then_inc(relu_ready, 1)

            split_hi(1, 0)
            k_high(0, 0, False)
            split_hi(1, 1)
            idx_high(0, ik_hi)
            idx_high(1, iq_hi[:, 0, :])
            split_hi(1, 2)
            relu_steps(0, 6)
            idx_high(2, iq_hi[:, 1, :])
            split_hi(1, 3)
            relu_steps(6, 12)
            idx_high(3, iq_hi[:, 2, :])
            split_hi(2, 0)
            relu_steps(12, 18)
            idx_high(4, iq_hi[:, 3, :])
            split_hi(2, 1)
            v_stage(0, 1)
            relu_steps(18, 24)
            split_hi(2, 2)
            gate_tanh(0, 1)
            split_hi(2, 3)

            body(0, 0, "fox")
            with act.Fori(1, 3) as g:
                body(g, g, "fox")
            with act.Fori(3, 7) as g:
                body(g, g, "dsa")
            last_body(7, 7, 9)

            def out_norms(layer, r, last):
                for j in (2, 3):
                    split_hi(r + 2, j)
                y_square(layer, 0)
                y_square(layer, 1)
                split_hi(r + 3, 0)
                if not last:
                    x_square(1, 0)
                split_hi(r + 3, 1)
                if not last:
                    x_square(1, 1)
                split_hi(r + 3, 2)
                split_hi(r + 3, 3)
                if not last:
                    h_high(1, 0)
                    h_high(1, 1)
                y_square(layer, 2)
                if not last:
                    split_hi(r + 4, 0)
                    split_hi(r + 4, 1)
                    split_hi(r + 4, 2)
                y_square(layer, 3)
                if not last:
                    x_square(1, 2)
                    split_hi(r + 4, 3)
                    x_square(1, 3)
                    h_high(1, 2)
                    h_high(1, 3)

            out_norms(0, 9, False)
            project(8, 13)
            with act.Fori(0, 7) as i:
                body(i + 8, i, "chk", 4)
            last_body(15, 7, 21)
            out_norms(1, 21, True)

        @block.vector
        def _(dve):
            st = Steps(dve, dve_steps)

            def split_lo(r, j, after_pool=False):
                if after_pool:
                    dve.wait_ge(w_lo_ready, 4 * r + j)
                dve.wait_ge(w_hi_ready, 4 * r + j + 1)
                dve.tensor_tensor(w_lo[:, j, :], w_raw[:, j, :], w_hi[:, j, :].bitcast(F32), ALU.subtract)\
                    .then_inc(w_lo_ready, 1)

            def x_scale(layer, t):
                dve.wait_ge(rstd_ready, NT * layer + t + 1)
                if t == 0:
                    dve.wait_ge(gpre_landed[layer], 16)
                if layer and t >= 2:
                    dve.wait_ge(xt_ready, 2 * (NT * layer + t - 1))
                dve.scalar_tensor_tensor(out=normed[layer][t], in0=xt[:, t, :], scalar=rstd[:, layer, 0, t:t + 1],
                                         in1=g_pre[:, :], op0=ALU.mult, op1=ALU.mult).then_inc(normed_ready, 1)

            def h_low(layer, t):
                for half in range(2):
                    dve.wait_ge(h_hi_ready, 2 * (NT * layer + t) + half + 1)
                    ks = slice(4 * half, 4 * half + 4)
                    dve.tensor_tensor(h_lo[:, ks, t * P:(t + 1) * P],
                                      tile_bank[t][half][:, :].rearrange("p (k s) -> p k s", k=4),
                                      h_hi[:, ks, t * P:(t + 1) * P].bitcast(F32),
                                      ALU.subtract).then_inc(h_lo_ready, 1)

            def y_scale(layer, t):
                dve.wait_ge(yrstd_ready, NT * layer + t + 1)
                if t == 0:
                    dve.wait_ge(gpost_landed, 16 * (layer + 1))
                for half in range(2):
                    cols = slice(half * S, (half + 1) * S)
                    ins = dve.scalar_tensor_tensor(out=y_normed[:, t % 2, cols], in0=tile_bank[t][half][:, :],
                                                   scalar=rstd[:, layer, 1, t:t + 1], in1=g_post[:, cols],
                                                   op0=ALU.mult, op1=ALU.mult)
                ins.then_inc(y_read, 1)
                dve.wait_ge(y_read, NT * layer + t + 1)
                dve.tensor_tensor(xt[:, t, :], xt[:, t, :], y_normed[:, t % 2, :], ALU.add).then_inc(x_added, 1)

            def rope(src, scale, dst=rope_b):
                alone(dve)
                st.done(dve.stream_shuffle(rope_a[:, :], src, SWAP))
                a = st.mark(dve.scalar_tensor_tensor(out=rope_a[:, :], in0=rope_a[:, :], scalar=scale,
                                                     in1=sin_t[:, :], op0=ALU.mult, op1=ALU.mult))
                b = st.mark(dve.scalar_tensor_tensor(out=dst[:, :], in0=src, scalar=scale, in1=cos_t[:, :],
                                                     op0=ALU.mult, op1=ALU.mult))
                st.wait(b)
                return dve.tensor_tensor(dst[:, :], dst[:, :], rope_a[:, :], ALU.add)

            def q_low(a, r, rotary, src=proj_bank[0]):
                if rotary:
                    dve.wait_ge(unit_used, 4 * r + 1)
                    rope(proj_bank[0][:, :], SCALE).then_inc(roped, 1)
                    dve.wait_ge(roped, 2 * (a - 4) + 1)
                dve.wait_ge(q_hi_ready, a + 1)
                if rotary:
                    dve.tensor_tensor(q_lo[:, :], rope_b[:, :], q_hi[:, :].bitcast(F32), ALU.subtract)\
                        .then_inc(q_ready, 1)
                else:
                    dve.scalar_tensor_tensor(out=q_lo[:, :], in0=src[:, :], scalar=SCALE,
                                             in1=q_hi[:, :].bitcast(F32), op0=ALU.mult, op1=ALU.subtract)\
                        .then_inc(q_ready, 1)

            def k_low(a, r, rotary, src=proj_bank[1]):
                if rotary:
                    src = k_roped
                dve.wait_ge(k_hi_ready, a + 1)
                dve.tensor_tensor(k_lo[:, :], src[:, :], k_hi[:, :].bitcast(F32), ALU.subtract)\
                    .then_inc(k_ready, 1)

            def k_rope(a, r):
                dve.wait_ge(unit_used, 4 * r + 2)
                rope(proj_bank[1][:, :], 1.0, k_roped).then_inc(roped, 1)
                dve.wait_ge(roped, 2 * (a - 4) + 2)

            def gate_make(a):
                dve.wait_ge(tanh_ready, a + 1)
                wait_past(dve, mixed, a)
                dve.scalar_tensor_tensor(out=gate, in0=tanh_g, scalar=1.0, in1=proj_bank[1][:, :],
                                         op0=ALU.add, op1=ALU.mult).then_inc(gate_ready, 1)

            def score(g, n, kind):
                h, tiles = GROUPS[n]
                dve.wait_ge(scores_ready, 6 * g + n + 1)
                alone(dve)
                col = 0
                for t in tiles:
                    w = (t + 1) * P
                    if kind == "fox":
                        b = bias[:, h, 0:w]
                    elif kind == "chk":
                        b = bias[:, h, S - w:S]
                    else:
                        b = sel_bias[:, OFF[t]:OFF[t] + w]
                    ins = dve.tensor_tensor_reduce(probs[:, h, OFF[t]:OFF[t] + w], group_bank[n][:, col:col + w],
                                                   b, -1.0, BIG, ALU.add, ALU.min,
                                                   neg_max[:, 4 * h + t:4 * h + t + 1])
                    col += w
                ins.then_inc(scored, 1)

            def inverse(g, h):
                dve.wait_ge(exp_ready, 8 * g + 6 + 2 * h)
                dve.reciprocal(row_inv[:, 4 * h:4 * h + 4], row_sum[:, 4 * h:4 * h + 4]).then_inc(inv_ready, 1)

            def search(rounds):
                for _ in range(rounds):
                    found = []
                    for t in (1, 2, 3):
                        row = work[:, W_OFF[t]:W_OFF[t] + (t + 1) * P]
                        found.append(st.mark(dve.max(best8[:, t - 1, :], row)))
                    for t in (1, 2, 3):
                        row = work[:, W_OFF[t]:W_OFF[t] + (t + 1) * P]
                        st.wait(found[t - 1])
                        alone(dve)
                        last = st.mark(dve.match_replace(row, best8[:, t - 1, :], row, TAKEN))
                    st.wait(last)
                    alone(dve)

            def mix_pair(g):
                dve.wait_ge(pv_done, 2 * g + 2)
                wait_past(dve, mix_lo_ready, g)
                dve.wait_ge(gate_ready, g + 1)
                dve.scalar_tensor_tensor(out=mix[:, :], in0=pv_bank[:, :], scalar=0.5, in1=gate,
                                         op0=ALU.mult, op1=ALU.mult).then_inc(mixed, 1)

            def mix_low(g, pair):
                dve.wait_ge(mix_hi_ready, g + 1)
                dve.tensor_tensor(mix_lo[:, pair, :], mix[:, :], mix_hi[:, pair, :].bitcast(F32), ALU.subtract)\
                    .then_inc(mix_lo_ready, 1)

            def project(a, r):
                split_lo(r + 1, 0)
                q_low(a, r, False, bank[0])
                split_lo(r + 1, 1)
                k_low(a, r, False, bank[1])
                split_lo(r + 1, 2)
                gate_make(a)
                split_lo(r + 1, 3)

            def first_scores(g, kind):
                if kind == "fox":
                    dve.wait_ge(bias_landed, 16 * g + 16)
                if kind == "chk":
                    dve.wait_ge(bias_masked, g - 7)
                wait_past(dve, pt_ready, 6 * g)
                score(g, 0, kind)
                score(g, 1, kind)

            def body(g, pair, kind, nxt, shift=0, rounds=(0, 0, 0)):
                r = g + 2 + shift
                first_scores(g, kind)
                for n in range(2, 6):
                    score(g, n, kind)
                inverse(g, 0)
                inverse(g, 1)
                q_low(g + 1, r, nxt == "dsa")
                if nxt == "dsa":
                    k_rope(g + 1, r)
                search(rounds[0])
                split_lo(r + 1, 1, after_pool=True)
                k_low(g + 1, r, nxt == "dsa")
                search(rounds[1])
                split_lo(r + 1, 2)
                search(rounds[2])
                mix_pair(g)
                gate_make(g + 1)
                mix_low(g, pair)
                split_lo(r + 1, 3)

            def last_body(g, pair, kind, r):
                first_scores(g, kind)
                for n in range(2, 6):
                    score(g, n, kind)
                inverse(g, 0)
                inverse(g, 1)
                for j in range(4):
                    split_lo(r + 1, j)
                split_lo(r + 2, 0)
                mix_pair(g)
                mix_low(g, pair)
                split_lo(r + 2, 1)

            x_scale(0, 0)
            x_scale(0, 1)
            x_scale(0, 2)
            h_low(0, 0)
            x_scale(0, 3)
            h_low(0, 1)
            dve.wait_ge(ws_hi_ready, 1)
            dve.tensor_tensor(ws_lo[:, :, :], ws_raw, ws_hi[:, :, :].bitcast(F32), ALU.subtract)\
                .then_inc(ws_lo_ready, 1)
            h_low(0, 2)
            h_low(0, 3)
            split_lo(0, 0)
            split_lo(0, 1)
            dve.wait_ge(rope_landed, 32)
            st.done(dve.tensor_copy(angle, pos_i))
            st.done(dve.tensor_scalar(angle, angle, rope_c[:, 0:1], None, ALU.mult))

            sine_angle, cosine_angle = rope_b[:, :], rope_a[:, :]
            st.done(dve.tensor_scalar(turns, angle, 1.0 / TWO_PI, ROUND_MAGIC, ALU.mult, ALU.add))
            st.done(dve.tensor_scalar(turns, turns, -ROUND_MAGIC, None, ALU.add))
            st.done(dve.scalar_tensor_tensor(out=sine_angle, in0=turns, scalar=-PI_HI, in1=angle,
                                             op0=ALU.mult, op1=ALU.add))
            for part in (PI_MID, PI_LO):
                st.done(dve.scalar_tensor_tensor(out=sine_angle, in0=turns, scalar=-part, in1=sine_angle,
                                                 op0=ALU.mult, op1=ALU.add))
            dve.tensor_scalar(sine_angle, sine_angle, PI_MAX, -PI_MAX, ALU.min, ALU.max).then_inc(angle_ready, 1)
            dve.wait_ge(angle_ready, 1)
            st.done(dve.scalar_tensor_tensor(out=cosine_angle, in0=sine_angle, scalar=-1.0, in1=sine_angle,
                                             op0=ALU.mult, op1=ALU.min))
            dve.tensor_scalar(cosine_angle, cosine_angle, TWO_PI / 4, None, ALU.add).then_inc(angle_ready, 1)
            rows = slice(F_ROW, F_ROW + 8)
            dve.wait_ge(consts_landed, 16 * 6)
            dve.wait_ge(small_ready, 1)
            dve.tensor_scalar(fz, small[rows, :], b_f[rows, 0:1], None, ALU.add).then_inc(fz_ready, 1)

            dve.wait_ge(small_t_ready, 1)
            st.done(dve.tensor_copy(small_tok[:, :, :], bank[1][:, 0:NT * P]
                                    .rearrange("p (t c) -> p t c", t=NT)[:, :, 0:SMALL]))
            iw = small_tok[:, :, IW_ROW:IW_ROW + 8]
            st.done(dve.tensor_scalar(iw, iw, IDX_SCALE, None, ALU.mult))
            ik = small_tok[:, :, 0:HD]
            stat = [ik_stat[:, n, :] for n in range(4)]

            def spread(col):
                return ik_stat[:, col, :].rearrange("p (t o) -> p t o", o=1).to_broadcast([P, NT, HD])

            st.done(dve.tensor_reduce(stat[0], ik, AX.X, ALU.add))
            st.done(dve.tensor_scalar(stat[0], stat[0], 1.0 / HD, None, ALU.mult))
            st.done(dve.tensor_tensor(ik_c, ik, spread(0), ALU.subtract))
            st.done(dve.tensor_tensor(ik_sq, ik_c, ik_c, ALU.mult))
            st.done(dve.tensor_reduce(stat[1], ik_sq, AX.X, ALU.add))
            dve.tensor_scalar(stat[1], stat[1], 1.0 / HD, EPS, ALU.mult, ALU.add).then_inc(ik_var_ready, 1)
            q_low(0, 0, False)
            dve.wait_ge(ik_rstd_ready, 1)
            dve.tensor_tensor(ik_dup[:, :, 0, :], ik_c, spread(2), ALU.mult)
            dve.tensor_tensor(ik_dup[:, :, 1, :], ik_c, spread(2), ALU.mult).then_inc(ik_dup_ready, 1)
            split_lo(0, 2)
            dve.wait_ge(sine_ready, 2)
            dve.tensor_scalar(sin_t[:, :], sin_t[:, :], rope_c[:, 1:2], None, ALU.mult)
            st.done(dve.tensor_scalar(cos_t[:, :], cos_t[:, :], rope_c[:, 2:3], rope_c[:, 3:4], ALU.mult, ALU.add))

            def idx_rope(n, src):
                rope(src, 1.0, roped_buf[n % 2]).then_inc(i_roped, 1)

            def idx_low(n, hi, lo):
                dve.wait_ge(i_roped, n + 1)
                dve.wait_ge(i_hi_ready, n + 1)
                dve.tensor_tensor(lo, roped_buf[n % 2][:, :], hi.bitcast(F32), ALU.subtract).then_inc(i_lo_ready, 1)

            def query_rope(j):
                dve.wait_ge(unit_used, j + 3)
                if j > 0:
                    dve.wait_ge(i_lo_ready, j)
                idx_rope(j + 1, proj_bank[j % 2][:, :])

            def query_low(j):
                idx_low(j + 1, iq_hi[:, j, :], iq_lo[:, j, :])

            def index_steps(first, last):
                for s in range(first, last):
                    t, h = s % 3 + 1, s // 3
                    w = (t + 1) * P
                    row = work[:, W_OFF[t]:W_OFF[t] + w]
                    weight = small_tok[:, t, IW_ROW + h:IW_ROW + h + 1]
                    dve.wait_ge(relu_ready, s + 1)
                    if h == 0:
                        dve.tensor_scalar(row, relu[:, s % 2, 0:w], weight, None, ALU.mult).then_inc(relu_used, 1)
                    else:
                        dve.wait_ge(relu_used, s - 2)
                        dve.scalar_tensor_tensor(out=row, in0=relu[:, s % 2, 0:w], scalar=weight, in1=row,
                                                 op0=ALU.mult, op1=ALU.add).then_inc(relu_used, 1)

            k_low(0, 0, False)
            dve.wait_ge(ik_t_ready, 1)
            st.done(dve.tensor_scalar(ik_gained, bank[2][:, :], ik_gb[:, 0:1], ik_gb[:, 1:2], ALU.mult, ALU.add))
            idx_rope(0, ik_gained)
            split_lo(0, 3)
            idx_low(0, ik_hi, ik_lo)
            query_rope(0)
            split_lo(1, 0)
            query_low(0)
            index_steps(0, 6)
            query_rope(1)
            query_low(1)
            split_lo(1, 1)
            index_steps(6, 12)
            query_rope(2)
            query_low(2)
            left = EXT - TAB
            dve.tensor_copy(ext[:, left:EXT], tab[:, ::-1])
            dve.tensor_copy(ext[:, 0:left], tab[:, TAB - 1:TAB].to_broadcast([16, left])).then_inc(ext_ready, 1)
            st.done(dve.memset(ones8, 1.0))
            dve.wait_ge(fl_ready, 1)
            st.done(dve.tensor_scalar(fz, fz, 0.0, None, ALU.min))
            st.done(dve.tensor_tensor(fz, fa, fz, ALU.subtract))
            dve.tensor_tensor_scan(small[rows, :], ones8, fz, 0.0, ALU.mult, ALU.add).then_inc(neg_f_ready, 1)
            dve.wait_ge(neg_f_ready, 1)
            index_steps(12, 18)
            query_rope(3)
            query_low(3)
            index_steps(18, 24)
            split_lo(2, 2, after_pool=True)
            dve.wait_ge(relu_used, 24)
            for t in (1, 2, 3):
                end = W_OFF[t] + (t + 1) * P
                last = st.mark(dve.memset(work[0:CHUNK, end - CHUNK:end], NEG))
            gate_make(0)
            split_lo(2, 3)
            st.wait(last)

            rounds = (1, 2, 2)
            assert 3 * sum(rounds) + 1 == ROUNDS
            body(0, 0, "fox", "fox", rounds=rounds)
            with st.loop(2, 6 * sum(rounds)) as i:
                body(i + 1, i + 1, "fox", "fox", rounds=rounds)
            body(3, 3, "fox", "dsa", rounds=(0, 1, 0))
            for t in (1, 2, 3):
                w = (t + 1) * P
                last = st.mark(dve.tensor_scalar(sel_bias[:, OFF[t]:OFF[t] + w], work[:, W_OFF[t]:W_OFF[t] + w],
                                                 TAKEN, NEG, ALU.not_equal, ALU.mult))
            st.wait(last)
            dve.wait_ge(consts_ready, 1)
            with st.loop(3, 6) as i:
                body(i + 4, i + 4, "dsa", "dsa")
            last_body(7, 7, "dsa", 9)

            def out_norms(layer, r, last):
                for j in (2, 3):
                    split_lo(r + 2, j)
                y_scale(layer, 0)
                y_scale(layer, 1)
                for j in range(4):
                    split_lo(r + 3, j)
                    if not last and j < 2:
                        x_scale(1, j)
                if not last:
                    h_low(1, 0)
                    h_low(1, 1)
                if not last:
                    split_lo(r + 4, 0)
                y_scale(layer, 2)
                if not last:
                    split_lo(r + 4, 1)
                y_scale(layer, 3)
                if not last:
                    x_scale(1, 2)
                    x_scale(1, 3)
                    split_lo(r + 4, 3, after_pool=True)
                    h_low(1, 2)
                    h_low(1, 3)

            out_norms(0, 9, False)
            project(8, 13)
            with st.loop(7, 0) as i:
                body(i + 8, i, "chk", "chk", 4)
            last_body(15, 7, "chk", 21)
            out_norms(1, 21, True)

        @block.tensor
        def _(pe):
            def transpose_x(layer, t):
                pe.wait_ge(normed_ready, NT * layer + t + 1)
                if layer:
                    pe.wait_ge(y_read, t + 1)
                for half in range(2):
                    for k in range(4):
                        src = normed[layer][t][:, (4 * half + k) * P:(4 * half + k + 1) * P]
                        ins = pe.transpose(tile_bank[t][half][:, k * P:(k + 1) * P], src, ident[:, :])
                    ins.then_inc(xt_ready, 1)

            def three_passes(dst, a_hi, a_lo, b_hi, b_lo, start, stop):
                pe.matmul(dst, a_hi, b_hi, start=start, stop=False)
                pe.matmul(dst, a_hi, b_lo, start=False, stop=False)
                return pe.matmul(dst, a_lo, b_hi, start=False, stop=stop)

            def unit(r, j, dst, first=0, last=S):
                pe.wait_ge(w_lo_ready, 4 * r + j + 1)
                toks = slice(first, last)
                for k in range(KT):
                    cols = slice(k * P, (k + 1) * P)
                    ins = three_passes(dst[:, toks], w_hi[:, j, cols], w_lo[:, j, cols], h_hi[:, k, toks],
                                       h_lo[:, k, toks], k == 0, k == KT - 1)
                if last == S:
                    ins.then_inc(unit_used, 1)

            def unit_q(a, r):
                wait_past(pe, v_staged, a)
                unit(r, 0, proj_bank[0])

            def unit_k(a, r):
                wait_past(pe, gate_ready, a)
                unit(r, 1, proj_bank[1])

            def unit_v(a, r, rotary=False):
                if rotary:
                    pe.wait_ge(roped, 2 * (a - 4) + 1)
                else:
                    pe.wait_ge(q_ready, a + 1)
                unit(r, 2, proj_bank[0])

            def unit_g(a, r, rotary=False):
                if rotary:
                    pe.wait_ge(roped, 2 * (a - 4) + 2)
                else:
                    pe.wait_ge(k_ready, a + 1)
                unit(r, 3, proj_bank[1])

            def turn_v(a):
                pe.wait_ge(v_staged, a + 1)
                wait_past(pe, scored, 6 * a)
                for t in range(NT):
                    ins = pe.transpose(score_bank[2][:, t * P:(t + 1) * P], v_t[:, t * P:(t + 1) * P], ident[:, :])
                ins.then_inc(vt_ready, 1)

            def scores(g, n, kind):
                h, tiles = GROUPS[n]
                if n == 2:
                    pe.wait_ge(v_ready, g + 1)
                if n in (3, 4):
                    pe.wait_ge(scored, 6 * g + n - 2)
                rows, col = slice(HD * h, HD * h + HD), 0
                for t in tiles:
                    w = (t + 1) * P
                    dst, cols = group_bank[n], slice(t * P, (t + 1) * P)
                    ins = three_passes(dst[:, col:col + w], q_hi[rows, cols], q_lo[rows, cols],
                                       k_hi[rows, 0:w], k_lo[rows, 0:w], True, kind != "fox")
                    if kind == "fox":
                        ins = pe.matmul(dst[:, col + w - P:col + w], ident_b[:, :], causal_b[:, :],
                                        start=False, stop=True)
                    col += w
                ins.then_inc(scores_ready, 1)

            def turn_probs(g, h):
                pe.wait_ge(probs_ready, 8 * g + 4 * h + 4)
                if h == 0:
                    pe.wait_ge(scored, 6 * g + 6)
                wait_past(pe, pt_read, 6 * g + 3 * h)
                for n, keys in enumerate(([0], [1], [2, 3])):
                    if n == 2 and turn_bank(g, h, n) is score_bank[h]:
                        pe.wait_ge(scored, 6 * g + 4 + h)
                    elif n == 2:
                        pe.wait_ge(scored, 6 * g + 3)
                    col = 0
                    for k in keys:
                        for t in range(k, NT):
                            ins = pe.transpose(turn_bank(g, h, n)[:, col:col + P],
                                               probs[:, h, OFF[t] + k * P:OFF[t] + (k + 1) * P], ident[:, :])
                            col += P
                    ins.then_inc(pt_ready, 1)

            def weigh_v(g, h):
                pe.wait_ge(pt_read, 6 * g + 3 * h + 3)
                if h == 0:
                    wait_past(pe, mixed, g)
                    pe.wait_ge(v_ready, g + 1)
                rows = slice(HD * h, HD * h + HD)
                for k in range(NT):
                    ins = pe.matmul(pv_bank[rows, k * P:S], v[:, k, rows], probs_t[:, h, KOFF[k]:KOFF[k] + S - k * P],
                                    start=(k == 0), stop=(k == NT - 1))
                ins.then_inc(pv_done, 1)

            def first_scores(g, kind):
                pe.wait_ge(k_ready, g + 1)
                pe.wait_ge(q_ready, g + 1)
                scores(g, 0, kind)
                scores(g, 1, kind)
                turn_v(g)

            def body(g, kind, nxt, shift=0):
                r = g + 2 + shift
                first_scores(g, kind)
                unit_q(g + 1, r)
                for n in range(2, 6):
                    scores(g, n, kind)
                unit_k(g + 1, r)
                turn_probs(g, 0)
                unit_v(g + 1, r, nxt == "dsa")
                weigh_v(g, 0)
                turn_probs(g, 1)
                unit_g(g + 1, r, nxt == "dsa")
                weigh_v(g, 1)

            def last_body(g, kind, layer, r):
                first_scores(g, kind)
                out_part(layer, r, 0, 0, 0)
                out_part(layer, r, 1, 0, 0)
                pe.wait_ge(gate_ready, g + 1)
                out_part(layer, r, 0, 0, 1)
                out_part(layer, r, 1, 0, 1)
                scores(g, 2, kind)
                scores(g, 3, kind)
                out_tile(layer, r, 2, 0)
                scores(g, 4, kind)
                scores(g, 5, kind)
                out_tile(layer, r, 3, 0)
                pe.wait_ge(scored, 6 * g + 5)
                out_tile(layer, r, 0, 1)
                out_tile(layer, r, 1, 1)
                turn_probs(g, 0)
                out_tile(layer, r, 2, 1)
                out_tile(layer, r, 3, 1)
                weigh_v(g, 0)
                turn_probs(g, 1)
                out_unit(layer, r + 1, 4)
                out_unit(layer, r + 1, 5)
                weigh_v(g, 1)
                out_unit(layer, r + 1, 6)
                out_unit(layer, r + 1, 7)

            def out_part(layer, r, k, t, n):
                j, toks, cols = k % 4, slice(t * P, (t + 1) * P), slice(n * S, (n + 1) * S)
                pe.wait_ge(w_lo_ready, 4 * r + j + 1)
                pe.wait_ge(mix_lo_ready, PAIRS * layer + k + 1)
                return three_passes(tile_bank[t][n][:, :], mix_hi[:, k, toks], mix_lo[:, k, toks],
                                    w_hi[:, j, cols], w_lo[:, j, cols], k == 0, k == KT - 1)

            def out_tile(layer, r, k, t):
                out_part(layer, r, k, t, 0)
                ins = out_part(layer, r, k, t, 1)
                if t % 2 == 1:
                    ins.then_inc(unit_used, 1)
                elif k == KT - 1:
                    ins.then_inc(y_ready, 1)

            def out_unit(layer, r, k):
                half = (r - (9, 21)[layer]) // 2
                out_tile(layer, r, k, 2 * half)
                out_tile(layer, r, k, 2 * half + 1)

            def second_half(layer, r):
                pe.wait_ge(pt_read, 48 * (layer + 1))
                pe.wait_ge(mixed, 8 * (layer + 1))
                for k in range(4):
                    out_unit(layer, r, k)
                for k in range(4, KT):
                    out_tile(layer, r + 1, k, 2)
                    if layer == 0 and k in (5, 6):
                        transpose_x(1, k - 5)
                for k in range(4, KT):
                    out_tile(layer, r + 1, k, 3)

            pe.wait_ge(consts_ready, 1)
            for t in range(NT):
                transpose_x(0, t)
            pe.wait_ge(ws_lo_ready, 1)
            for half in range(2):
                pe.wait_ge(h_lo_ready, NT * (half + 1))
                toks = slice(half * S // 2, (half + 1) * S // 2)
                for k in range(KT):
                    ins = three_passes(bank[0][0:SMALL, toks], ws_hi[:, k, :], ws_lo[:, k, :], h_hi[:, k, toks],
                                       h_lo[:, k, toks], k == 0, k == KT - 1)
            ins.then_inc(small_done, 1)
            unit(0, 0, proj_bank[0])
            pe.wait_ge(small_ready, 1)
            for t in range(NT):
                ins = pe.transpose(bank[1][:, t * P:t * P + SMALL], small[:, t * P:(t + 1) * P],
                                   ident[0:SMALL, 0:SMALL])
            ins.then_inc(small_t_ready, 1)
            unit(0, 1, proj_bank[1])

            pe.wait_ge(ik_dup_ready, 1)
            for t in range(NT):
                ins = pe.transpose(bank[2][:, t * P:(t + 1) * P], ik_dup[:, t, :, :].rearrange("p c d -> p (c d)"),
                                   ident[:, :])
            ins.then_inc(ik_t_ready, 1)
            pe.wait_ge(q_ready, 1)
            unit(0, 2, proj_bank[0])
            pe.wait_ge(k_ready, 1)
            unit(0, 3, proj_bank[1])

            def index_scores(j):
                pe.wait_ge(i_lo_ready, j + 2)
                for s in range(6 * j, 6 * j + 6):
                    t, h = s % 3 + 1, s // 3
                    if s >= 3:
                        pe.wait_ge(relu_ready, s - 2)
                    rows, w, cols = slice(HD * (h % 2), HD * (h % 2) + HD), (t + 1) * P, slice(t * P, (t + 1) * P)
                    three_passes(score_bank[s % 3][:, 0:w], iq_hi[rows, j, cols], iq_lo[rows, j, cols],
                                 ik_hi[rows, 0:w], ik_lo[rows, 0:w], True, True).then_inc(idx_ready, 1)

            index_scores(0)
            pe.wait_ge(i_roped, 2)
            unit(1, 0, proj_bank[0])
            index_scores(1)
            pe.wait_ge(i_roped, 3)
            unit(1, 1, proj_bank[1])
            index_scores(2)
            pe.wait_ge(i_roped, 4)
            unit(1, 2, proj_bank[0])
            index_scores(3)
            pe.wait_ge(i_roped, 5)
            unit(1, 3, proj_bank[1])
            pe.wait_ge(relu_ready, 24)

            body(0, "fox", "fox")
            with pe.Fori(1, 3) as g:
                body(g, "fox", "fox")
            body(3, "fox", "dsa")
            with pe.Fori(4, 7) as g:
                body(g, "dsa", "dsa")
            last_body(7, "dsa", 0, 9)
            second_half(0, 11)

            pe.wait_ge(h_lo_ready, 3 * NT)
            first_banks = (bank[0], bank[1], proj_bank[0], proj_bank[1])
            for j in range(4):
                unit(13, j, first_banks[j], 0, S // 2)
                if j >= 2:
                    transpose_x(1, j)
            pe.wait_ge(h_lo_ready, 4 * NT)
            for j in range(4):
                unit(13, j, first_banks[j], S // 2, S)
            with pe.Fori(8, 15) as g:
                body(g, "chk", "chk", 4)
            last_body(15, "chk", 1, 21)
            second_half(1, 23)


def unit_columns(w, first, width, pair):
    cols = w[:, first + pair * P:first + pair * P + P]
    return cols.reshape(KT, P, P).transpose(1, 0, 2).reshape(P, KT * P)


def kernel(x, positions, pre_norm_g, post_norm_g, w_in_even, b_forget, idx_k_g, idx_k_b,
           w_out_even, w_in_odd, rel_bias, w_out_odd):
    import concourse.bacc as bacc
    from concourse.bass_utils import run_bass_kernel_spmd

    w0, w1 = np.asarray(w_in_even)[0], np.asarray(w_in_odd)[0]
    fq, fk, fv, ff, fg = 0, 512, 1024, 1536, 1544
    dq, dk, dv, iq, ik, iw, dg = 2056, 2568, 3080, 3592, 4104, 4168, 4176
    units = [unit_columns(w0, c, P, 0) for c in (fq, fk)]
    units += [unit_columns(w0, iq, P, j) for j in range(IDX_UNITS)]
    units += [unit_columns(w0, c, P, 0) for c in (fv, fg)]
    units += [unit_columns(w0, c, P, p) for p in (1, 2, 3) for c in (fq, fk, fv, fg)]
    units += [unit_columns(w0, c, P, p) for p in range(4) for c in (dq, dk, dv, dg)]
    units += [np.asarray(w_out_even)[0, k * P:(k + 1) * P] for k in range(KT)]
    units += [unit_columns(w1, c, P, p) for p in range(PAIRS) for c in (0, D, 2 * D, 3 * D)]
    units += [np.asarray(w_out_odd)[0, k * P:(k + 1) * P] for k in range(KT)]
    small = np.concatenate([w0[:, ik:ik + HD], w0[:, ff:ff + 8], w0[:, iw:iw + 8]], axis=1)
    small = small.reshape(KT, P, SMALL).transpose(1, 0, 2).reshape(P, KT * SMALL)

    row = np.arange(P) % HD
    rotated = row < ROT
    freq = (THETA ** (-np.arange(0, ROT, 2) / ROT)).astype(np.float32)
    rope_consts = np.stack([np.where(rotated, freq[row % (ROT // 2)], 0),
                            np.where(rotated, np.where(row < ROT // 2, -1, 1), 0),
                            rotated, ~rotated], axis=1).astype(np.float32)

    arrays = {
        "x": np.ascontiguousarray(np.asarray(x)[0]),
        "positions": np.ascontiguousarray(np.asarray(positions)),
        "pre_g": np.ascontiguousarray(pre_norm_g),
        "post_g": np.ascontiguousarray(post_norm_g),
        "w_units": np.ascontiguousarray(np.stack(units)),
        "w_small": np.ascontiguousarray(small),
        "b_forget": np.ascontiguousarray(np.asarray(b_forget).reshape(8, 1)),
        "idx_g": np.ascontiguousarray(np.asarray(idx_k_g).reshape(HD, 1)),
        "idx_b": np.ascontiguousarray(np.asarray(idx_k_b).reshape(HD, 1)),
        "rel_bias": np.ascontiguousarray(np.asarray(rel_bias)[0]),
        "rope_consts": rope_consts,
    }
    nc = bacc.Bacc("TRN2", target_bir_lowering=False, num_devices=1)
    args = [nc.dram_tensor(n, a.shape, mybir.dt.from_np(a.dtype), kind="ExternalInput").ap()
            for n, a in arrays.items()]
    out = nc.dram_tensor("out", (S, D), F32, kind="ExternalOutput").ap()
    neg_f_dram = nc.dram_tensor("neg_f", (4, 2 * S), F32, kind="Internal").ap()
    ext_dram = nc.dram_tensor("ext", (PAIRS, 2 * P * EXT), F32, kind="Internal").ap()
    trunk_program(nc, *args, out, neg_f_dram, ext_dram)
    r = run_bass_kernel_spmd(nc, [arrays], core_ids=[0])
    return r.results[0]["out"].reshape(1, S, D)
```
